# Optimizing a Trainium2 kernel written in Bass

```python
import jax, jax.numpy as jnp
from jax import lax
import numpy as np

D_MODEL = 1024
BATCH = 1
SEQ = 256
DEPTH = 1

EPS = 1e-6
GRID_W = 64
D_MIX = D_MODEL

GLA_HEADS = 4
GLA_DK = 64
GLA_DV = 128
GLA_KEY_WIDTH = GLA_HEADS * GLA_DK
GLA_WIDTH = GLA_HEADS * GLA_DV
GLA_GATE_RANK = 16
GLA_GATE_NORM = 16.0
GLA_CHUNK = 64

ATT_HEADS = 8
ATT_KV_HEADS = 2
ATT_HEAD_DIM = 64
ATT_WIDTH = ATT_HEADS * ATT_HEAD_DIM
ATT_KV_WIDTH = ATT_KV_HEADS * ATT_HEAD_DIM
Q_BLOCK = 128
ROPE_THETA = 10000.0

N_GROUPS = 8
EXPERTS_PER_GROUP = 8
N_EXPERTS = N_GROUPS * EXPERTS_PER_GROUP
TOP_K = 2
D_EXPERT = 512
MOE_BLOCK = 128

IN_SIZES = (GLA_KEY_WIDTH, GLA_KEY_WIDTH, GLA_WIDTH, GLA_WIDTH,
            GLA_GATE_RANK, GLA_GATE_RANK,
            ATT_WIDTH, ATT_KV_WIDTH, ATT_KV_WIDTH)
D_IN = 2336


def rms_norm(x, gain):
    x32 = x.astype(jnp.float32)
    y = x32 * lax.rsqrt(jnp.mean(x32 * x32, axis=-1, keepdims=True) + EPS)
    return y.astype(x.dtype) * gain

def gla_chunked(q, k, v, log_a):
    B, H, T, dk = q.shape
    dv = v.shape[-1]
    C = GLA_CHUNK
    N = T // C
    f32 = jnp.float32
    qf = q.astype(f32).reshape(B, H, N, C, dk)
    kf = k.astype(f32).reshape(B, H, N, C, dk)
    vf = v.astype(f32).reshape(B, H, N, C, dv)
    b = jnp.cumsum(log_a.astype(f32).reshape(B, H, N, C, dk), axis=3)
    b_ref = b[:, :, :, C // 2 - 1:C // 2, :]
    b_last = b[:, :, :, -1:, :]
    scores = jnp.einsum('bhncd,bhnsd->bhncs', qf * jnp.exp(b - b_ref), kf * jnp.exp(b_ref - b))
    mask = jnp.tril(jnp.ones((C, C), dtype=bool))
    scores = jnp.where(mask, scores, 0.0)
    o_intra = jnp.einsum('bhncs,bhnse->bhnce', scores, vf)
    chunk_kv = jnp.einsum('bhncd,bhnce->bhnde', kf * jnp.exp(b_last - b), vf)
    chunk_decay = jnp.exp(b_last[:, :, :, 0, :])

    def step(state, inp):
        decay, kv = inp
        return decay[..., None] * state + kv, state

    init = jnp.zeros((B, H, dk, dv), f32)
    _, states = lax.scan(step, init, (jnp.moveaxis(chunk_decay, 2, 0), jnp.moveaxis(chunk_kv, 2, 0)))
    states = jnp.moveaxis(states, 0, 2)
    o_inter = jnp.einsum('bhncd,bhnde->bhnce', qf * jnp.exp(b), states)
    return (o_intra + o_inter).reshape(B, H, T, dv).astype(v.dtype)

def gla_group(q, k, v, g, z_fwd, z_bwd, up_f, up_f_bias, up_b, up_b_bias, out_gain):
    B, T, _ = q.shape

    def heads(t, d):
        return t.reshape(B, T, GLA_HEADS, d).transpose(0, 2, 1, 3)

    qh = heads(q, GLA_DK) * (GLA_DK ** -0.5)
    kh = heads(k, GLA_DK)
    vh = heads(v, GLA_DV)
    la_f = heads(jax.nn.log_sigmoid((z_fwd @ up_f + up_f_bias).astype(jnp.float32)) / GLA_GATE_NORM, GLA_DK)
    la_b = heads(jax.nn.log_sigmoid((z_bwd @ up_b + up_b_bias).astype(jnp.float32)) / GLA_GATE_NORM, GLA_DK)
    o_f = gla_chunked(qh, kh, vh, la_f)
    flip = lambda t: jnp.flip(t, axis=2)
    o_b = flip(gla_chunked(flip(qh), flip(kh), flip(vh), flip(la_b)))
    o = rms_norm(o_f + o_b, out_gain)
    o = o.transpose(0, 2, 1, 3).reshape(B, T, GLA_WIDTH)
    return o * jax.nn.silu(g)

def axial_rope_tables(T):
    rows = T // GRID_W
    row = jnp.repeat(jnp.arange(rows), GRID_W).astype(jnp.float32)
    col = jnp.tile(jnp.arange(GRID_W), rows).astype(jnp.float32)
    axis_dim = ATT_HEAD_DIM // 2
    inv_freq = ROPE_THETA ** (-jnp.arange(0, axis_dim, 2, dtype=jnp.float32) / axis_dim)
    ang = jnp.concatenate([row[:, None] * inv_freq, col[:, None] * inv_freq], axis=-1)
    return jnp.cos(ang), jnp.sin(ang)

def apply_axial_rope(x, cos, sin):
    xr = x.astype(jnp.float32).reshape(*x.shape[:-1], -1, 2)
    x0, x1 = xr[..., 0], xr[..., 1]
    out = jnp.stack([x0 * cos - x1 * sin, x0 * sin + x1 * cos], axis=-1)
    return out.reshape(x.shape).astype(x.dtype)

def gqa_group(q, k, v, q_gain, k_gain, out_gain):
    B, T, _ = q.shape
    dh = ATT_HEAD_DIM
    G = ATT_HEADS // ATT_KV_HEADS
    qh = rms_norm(q.reshape(B, T, ATT_HEADS, dh).transpose(0, 2, 1, 3), q_gain)
    kh = rms_norm(k.reshape(B, T, ATT_KV_HEADS, dh).transpose(0, 2, 1, 3), k_gain)
    vh = v.reshape(B, T, ATT_KV_HEADS, dh).transpose(0, 2, 1, 3)
    cos, sin = axial_rope_tables(T)
    qh = apply_axial_rope(qh, cos, sin) * (dh ** -0.5)
    kh = apply_axial_rope(kh, cos, sin)
    nb = T // Q_BLOCK
    q_blocks = qh.reshape(B, ATT_KV_HEADS, G, nb, Q_BLOCK, dh).transpose(3, 0, 1, 2, 4, 5)

    def attend(qb):
        s = jnp.einsum('bkgqd,bksd->bkgqs', qb, kh).astype(jnp.float32)
        p = jax.nn.softmax(s, axis=-1).astype(vh.dtype)
        return jnp.einsum('bkgqs,bksd->bkgqd', p, vh)

    o = lax.map(attend, q_blocks)
    o = o.transpose(1, 0, 4, 2, 3, 5).reshape(B, T, ATT_WIDTH)
    return rms_norm(o, out_gain)

def hier_moe(x, w_group, b_group, w_expert, b_expert, w_gate, w_up, w_down):
    B, T, D = x.shape
    xt = x.reshape(-1, D)
    N = xt.shape[0]
    g_logits = (xt @ w_group + b_group).astype(jnp.float32)
    g_prob = jax.nn.softmax(g_logits, axis=-1)
    g_idx = jnp.argmax(g_logits, axis=-1)
    g_w = jnp.take_along_axis(g_prob, g_idx[:, None], axis=-1)
    e_logits = (xt @ w_expert + b_expert).astype(jnp.float32).reshape(N, N_GROUPS, EXPERTS_PER_GROUP)
    e_logits = jnp.take_along_axis(e_logits, g_idx[:, None, None], axis=1)[:, 0]
    top_val, top_idx = lax.top_k(e_logits, TOP_K)
    gate = g_w * jax.nn.softmax(top_val, axis=-1)
    expert_id = g_idx[:, None] * EXPERTS_PER_GROUP + top_idx

    M = N * TOP_K
    flat_e = expert_id.reshape(M).astype(jnp.int32)
    flat_tok = jnp.repeat(jnp.arange(N, dtype=jnp.int32), TOP_K)
    flat_gate = gate.reshape(M).astype(x.dtype)
    order = jnp.argsort(flat_e)
    se = flat_e[order]
    counts = jnp.bincount(flat_e, length=N_EXPERTS)
    starts = jnp.cumsum(counts) - counts
    padded = (counts + MOE_BLOCK - 1) // MOE_BLOCK * MOE_BLOCK
    pad_ends = jnp.cumsum(padded)
    pad_starts = pad_ends - padded
    dest = pad_starts[se] + (jnp.arange(M, dtype=jnp.int32) - starts[se])
    P = M + N_EXPERTS * MOE_BLOCK
    slot_tok = jnp.zeros((P,), jnp.int32).at[dest].set(flat_tok[order])
    slot_gate = jnp.zeros((P,), x.dtype).at[dest].set(flat_gate[order])
    nblk = P // MOE_BLOCK
    blk_start = jnp.arange(nblk, dtype=jnp.int32) * MOE_BLOCK
    blk_expert = jnp.minimum(jnp.searchsorted(pad_ends, blk_start, side='right'), N_EXPERTS - 1)
    xs = xt[slot_tok].reshape(nblk, MOE_BLOCK, D)

    def run_block(args):
        xb, e = args
        h = jax.nn.silu(xb @ w_gate[e]) * (xb @ w_up[e])
        return h @ w_down[e]

    ys = lax.map(run_block, (xs, blk_expert)).reshape(P, D)
    y = jnp.zeros((N, D), x.dtype).at[slot_tok].add(ys * slot_gate[:, None])
    return y.reshape(B, T, D)

def first_inputs(seed: int = 0) -> dict:
    key = jax.random.key(seed)
    ks = jax.random.split(key, 24)
    f32 = jnp.float32
    L = DEPTH

    def nrm(k, shape, scale):
        return jax.random.normal(k, shape, f32) * scale

    def gain(k, shape):
        return 1.0 + 0.02 * jax.random.normal(k, shape, f32)

    return {
        "x": nrm(ks[0], (BATCH, SEQ, D_MODEL), 1.0),
        "norm1_gain": gain(ks[1], (L, D_MODEL)),
        "w_in": nrm(ks[2], (L, D_MODEL, D_IN), D_MODEL ** -0.5),
        "gla_up_fwd": nrm(ks[3], (L, GLA_GATE_RANK, GLA_KEY_WIDTH), GLA_GATE_RANK ** -0.5),
        "gla_up_fwd_bias": nrm(ks[4], (L, GLA_KEY_WIDTH), 0.1),
        "gla_up_bwd": nrm(ks[5], (L, GLA_GATE_RANK, GLA_KEY_WIDTH), GLA_GATE_RANK ** -0.5),
        "gla_up_bwd_bias": nrm(ks[6], (L, GLA_KEY_WIDTH), 0.1),
        "gla_out_gain": gain(ks[7], (L, GLA_DV)),
        "q_norm_gain": gain(ks[8], (L, ATT_HEAD_DIM)),
        "k_norm_gain": gain(ks[9], (L, ATT_HEAD_DIM)),
        "att_out_gain": gain(ks[10], (L, ATT_WIDTH)),
        "w_out": nrm(ks[11], (L, D_MIX, D_MODEL), D_MIX ** -0.5),
        "norm2_gain": gain(ks[12], (L, D_MODEL)),
        "w_group": nrm(ks[13], (L, D_MODEL, N_GROUPS), D_MODEL ** -0.5),
        "b_group": nrm(ks[14], (L, N_GROUPS), 0.01),
        "w_expert": nrm(ks[15], (L, D_MODEL, N_EXPERTS), D_MODEL ** -0.5),
        "b_expert": nrm(ks[16], (L, N_EXPERTS), 0.01),
        "w_gate": nrm(ks[17], (L, N_EXPERTS, D_MODEL, D_EXPERT), D_MODEL ** -0.5),
        "w_up": nrm(ks[18], (L, N_EXPERTS, D_MODEL, D_EXPERT), D_MODEL ** -0.5),
        "w_down": nrm(ks[19], (L, N_EXPERTS, D_EXPERT, D_MODEL), D_EXPERT ** -0.5),
        "final_gain": gain(ks[20], (D_MODEL,)),
    }

def first_block(x, norm1_gain, w_in, gla_up_fwd, gla_up_fwd_bias, gla_up_bwd, gla_up_bwd_bias,
              gla_out_gain, q_norm_gain, k_norm_gain, att_out_gain, w_out, norm2_gain,
              w_group, b_group, w_expert, b_expert, w_gate, w_up, w_down, final_gain):
    split_points = np.cumsum(IN_SIZES)[:-1].tolist()
    h = x
    for l in range(DEPTH):
        u = rms_norm(h, norm1_gain[l])
        proj = u @ w_in[l]
        gq, gk, gv, gg, zf, zb, aq, ak, av = jnp.split(proj, split_points, axis=-1)
        o_gla = gla_group(gq, gk, gv, gg, zf, zb, gla_up_fwd[l], gla_up_fwd_bias[l],
                          gla_up_bwd[l], gla_up_bwd_bias[l], gla_out_gain[l])
        o_att = gqa_group(aq, ak, av, q_norm_gain[l], k_norm_gain[l], att_out_gain[l])
        mixed = jnp.concatenate([o_gla, o_att], axis=-1)
        h = h + mixed @ w_out[l]
        h = h + hier_moe(rms_norm(h, norm2_gain[l]), w_group[l], b_group[l], w_expert[l],
                         b_expert[l], w_gate[l], w_up[l], w_down[l])
    return rms_norm(h, final_gain)


N_MEM = 256
NORM_EPS = 1e-6
NEG_INF = -1e30

MIX_WIDTH = D_MODEL
MOBA_WIDTH = MIX_WIDTH // 2
RET_WIDTH = MIX_WIDTH - MOBA_WIDTH

MOBA_HEAD_DIM = 64
MOBA_HEADS = MOBA_WIDTH // MOBA_HEAD_DIM
MOBA_BLOCK = 256
MOBA_TOPK = 3
MOBA_Q_BLOCK = 32
ROPE_THETA_2 = 500000.0
ROPE_DIM = MOBA_HEAD_DIM // 4

RET_HEADS = 4
RET_V_DIM = RET_WIDTH // RET_HEADS
RET_QK_DIM = RET_V_DIM // 2
RET_CHUNK = 128
RET_THETA = 10000.0

CROSS_HEADS = 4
CROSS_HEAD_DIM = D_MODEL // CROSS_HEADS

D_FF = -(-8 * D_MODEL // (3 * 256)) * 256

W_MQ = MOBA_WIDTH
W_MK = MOBA_WIDTH
W_MV = MOBA_WIDTH
W_RQ = RET_HEADS * RET_QK_DIM
W_RK = RET_HEADS * RET_QK_DIM
W_RV = RET_WIDTH
W_RG = RET_WIDTH
IN_PROJ_WIDTH = W_MQ + W_MK + W_MV + W_RQ + W_RK + W_RV + W_RG
SPLIT_POINTS = [W_MQ, W_MQ + W_MK, W_MQ + W_MK + W_MV,
                W_MQ + W_MK + W_MV + W_RQ,
                W_MQ + W_MK + W_MV + W_RQ + W_RK,
                W_MQ + W_MK + W_MV + W_RQ + W_RK + W_RV]


def rms_norm_2(x, g):
    xf = x.astype(jnp.float32)
    y = xf * lax.rsqrt(jnp.mean(xf * xf, axis=-1, keepdims=True) + NORM_EPS)
    return (y * g.astype(jnp.float32)).astype(x.dtype)

def rotary(x, inv_freq, rot_dim):
    S = x.shape[2]
    half = rot_dim // 2
    ang = jnp.arange(S, dtype=jnp.float32)[:, None] * inv_freq[None, :]
    cos, sin = jnp.cos(ang), jnp.sin(ang)
    xr = x[..., :rot_dim].astype(jnp.float32)
    x1, x2 = xr[..., :half], xr[..., half:]
    rot = jnp.concatenate([x1 * cos - x2 * sin, x2 * cos + x1 * sin], axis=-1).astype(x.dtype)
    return jnp.concatenate([rot, x[..., rot_dim:]], axis=-1)

def split_heads(t, n_heads):
    B, S, _ = t.shape
    return t.reshape(B, S, n_heads, -1).transpose(0, 2, 1, 3)

def merge_heads(t):
    B, H, S, d = t.shape
    return t.transpose(0, 2, 1, 3).reshape(B, S, H * d)

def moba_attention(q, k, v):
    B, H, S, dh = q.shape
    L = MOBA_BLOCK
    nb = -(-S // L)
    pad = nb * L - S
    kp = jnp.pad(k, ((0, 0), (0, 0), (0, pad), (0, 0)))
    vp = jnp.pad(v, ((0, 0), (0, 0), (0, pad), (0, 0)))
    k_blocks = kp.reshape(B, H, nb, L, dh)
    v_blocks = vp.reshape(B, H, nb, L, dh)
    k_mean = jnp.mean(k_blocks.astype(jnp.float32), axis=3).astype(q.dtype)
    n_sel = min(MOBA_TOPK, nb)
    scale = dh ** -0.5
    QB = MOBA_Q_BLOCK
    nq = S // QB
    q_blocks = q.reshape(B, H, nq, QB, dh).transpose(2, 0, 1, 3, 4)
    b_idx = jnp.arange(B)[:, None, None, None]
    h_idx = jnp.arange(H)[None, :, None, None]
    block_ids = jnp.arange(nb)
    slot_ids = jnp.arange(n_sel)
    key_offsets = jnp.arange(L)

    def one_query_block(args):
        qb, qi = args
        q_pos = qi * QB + jnp.arange(QB)
        cur = (qi * QB) // L
        gate = jnp.einsum('bhqd,bhnd->bhqn', qb, k_mean).astype(jnp.float32)
        gate = jnp.where((block_ids < cur)[None, None, None, :], gate, NEG_INF)
        _, sel = lax.top_k(gate, n_sel)
        slot_valid = slot_ids < cur
        k_sel = k_blocks[b_idx, h_idx, sel]
        v_sel = v_blocks[b_idx, h_idx, sel]
        s_sel = jnp.einsum('bhqd,bhqnld->bhqnl', qb, k_sel).astype(jnp.float32) * scale
        s_sel = jnp.where(slot_valid[:, None], s_sel, NEG_INF)
        k_own = lax.dynamic_index_in_dim(k_blocks, cur, axis=2, keepdims=False)
        v_own = lax.dynamic_index_in_dim(v_blocks, cur, axis=2, keepdims=False)
        s_own = jnp.einsum('bhqd,bhld->bhql', qb, k_own).astype(jnp.float32) * scale
        own_pos = cur * L + key_offsets
        s_own = jnp.where(own_pos[None, :] <= q_pos[:, None], s_own, NEG_INF)
        logits = jnp.concatenate([s_sel.reshape(B, H, QB, n_sel * L), s_own], axis=-1)
        p = jax.nn.softmax(logits, axis=-1)
        p_sel = p[..., :n_sel * L].reshape(B, H, QB, n_sel, L).astype(v.dtype)
        p_own = p[..., n_sel * L:].astype(v.dtype)
        return (jnp.einsum('bhqnl,bhqnld->bhqd', p_sel, v_sel)
                + jnp.einsum('bhql,bhld->bhqd', p_own, v_own))

    out = lax.map(one_query_block, (q_blocks, jnp.arange(nq)))
    return out.transpose(1, 2, 0, 3, 4).reshape(B, H, S, dh)

def retention(q, k, v):
    B, H, S, dk = q.shape
    dv = v.shape[-1]
    C = RET_CHUNK
    nc = S // C
    log_g = jnp.log(1.0 - jnp.power(2.0, -5.0 - jnp.arange(H, dtype=jnp.float32)))
    idx = jnp.arange(C, dtype=jnp.float32)
    diff = idx[:, None] - idx[None, :]
    inner_decay = jnp.where(diff >= 0, jnp.exp(log_g[:, None, None] * jnp.maximum(diff, 0.0)), 0.0)
    q_decay = jnp.exp(log_g[:, None] * (idx + 1.0))[None, :, :, None]
    k_decay = jnp.exp(log_g[:, None] * (C - 1.0 - idx))[None, :, :, None]
    chunk_decay = jnp.exp(log_g * C)[None, :, None, None]

    def to_chunks(t):
        return t.astype(jnp.float32).reshape(B, H, nc, C, t.shape[-1]).transpose(2, 0, 1, 3, 4)

    def step(state, inp):
        qc, kc, vc = inp
        attn = jnp.einsum('bhid,bhjd->bhij', qc, kc) * inner_decay[None]
        inner = jnp.einsum('bhij,bhjv->bhiv', attn, vc)
        cross = jnp.einsum('bhid,bhdv->bhiv', qc * q_decay, state)
        new_state = state * chunk_decay + jnp.einsum('bhjd,bhjv->bhdv', kc * k_decay, vc)
        return new_state, inner + cross

    state0 = jnp.zeros((B, H, dk, dv), jnp.float32)
    _, out = lax.scan(step, state0, (to_chunks(q), to_chunks(k), to_chunks(v)))
    return out.transpose(1, 2, 0, 3, 4).reshape(B, H, S, dv)

def cross_attention(h, mem_n, w_cq, w_ckv, w_co):
    q = split_heads(h @ w_cq, CROSS_HEADS)
    kv = mem_n @ w_ckv
    k = split_heads(kv[..., :D_MODEL], CROSS_HEADS)
    v = split_heads(kv[..., D_MODEL:], CROSS_HEADS)
    s = jnp.einsum('bhsd,bhmd->bhsm', q, k).astype(jnp.float32) * (CROSS_HEAD_DIM ** -0.5)
    p = jax.nn.softmax(s, axis=-1).astype(v.dtype)
    o = jnp.einsum('bhsm,bhmd->bhsd', p, v)
    return merge_heads(o) @ w_co

def second_inputs(seed: int = 0) -> dict:
    key = jax.random.key(seed)
    ks = jax.random.split(key, 16)

    def w(k, shape, fan_in):
        return jax.random.normal(k, shape, jnp.float32) * (fan_in ** -0.5)

    def gain(k):
        return 1.0 + 0.05 * jax.random.normal(k, (DEPTH, D_MODEL), jnp.float32)

    return {
        "x": jax.random.normal(ks[0], (BATCH, SEQ, D_MODEL), jnp.float32),
        "mem": jax.random.normal(ks[1], (BATCH, N_MEM, D_MODEL), jnp.float32),
        "g_pre_mix": gain(ks[2]),
        "w_in": w(ks[3], (DEPTH, D_MODEL, IN_PROJ_WIDTH), D_MODEL),
        "w_out": w(ks[4], (DEPTH, MIX_WIDTH, D_MODEL), MIX_WIDTH),
        "g_post_mix": gain(ks[5]),
        "g_pre_cross": gain(ks[6]),
        "g_mem": gain(ks[7]),
        "w_cq": w(ks[8], (DEPTH, D_MODEL, D_MODEL), D_MODEL),
        "w_ckv": w(ks[9], (DEPTH, D_MODEL, 2 * D_MODEL), D_MODEL),
        "w_co": w(ks[10], (DEPTH, D_MODEL, D_MODEL), D_MODEL),
        "g_post_cross": gain(ks[11]),
        "g_pre_ffn": gain(ks[12]),
        "w_gate_up": w(ks[13], (DEPTH, D_MODEL, 2 * D_FF), D_MODEL),
        "w_down": w(ks[14], (DEPTH, D_FF, D_MODEL), D_FF),
        "g_post_ffn": gain(ks[15]),
    }

def second_block(x, mem, g_pre_mix, w_in, w_out, g_post_mix, g_pre_cross, g_mem, w_cq, w_ckv,
              w_co, g_post_cross, g_pre_ffn, w_gate_up, w_down, g_post_ffn):
    moba_inv = jnp.power(ROPE_THETA_2, -jnp.arange(ROPE_DIM // 2, dtype=jnp.float32) * 2.0 / ROPE_DIM)
    ret_inv = 1.0 / jnp.power(RET_THETA, jnp.linspace(0.0, 1.0, RET_QK_DIM // 2, dtype=jnp.float32))
    for l in range(DEPTH):
        h = rms_norm_2(x, g_pre_mix[l])
        proj = h @ w_in[l]
        mq, mk, mv, rq, rk, rv, rg = jnp.split(proj, SPLIT_POINTS, axis=-1)
        mq = rotary(split_heads(mq, MOBA_HEADS), moba_inv, ROPE_DIM)
        mk = rotary(split_heads(mk, MOBA_HEADS), moba_inv, ROPE_DIM)
        mo = merge_heads(moba_attention(mq, mk, split_heads(mv, MOBA_HEADS)))
        rq = rotary(split_heads(rq, RET_HEADS), ret_inv, RET_QK_DIM)
        rk = rotary(split_heads(rk, RET_HEADS), ret_inv, RET_QK_DIM) * (RET_QK_DIM ** -0.5)
        ro = retention(rq, rk, split_heads(rv, RET_HEADS))
        ro = ro * lax.rsqrt(jnp.mean(ro * ro, axis=-1, keepdims=True) + NORM_EPS)
        ro = jax.nn.silu(rg) * merge_heads(ro).astype(x.dtype)
        mix = jnp.concatenate([mo, ro], axis=-1) @ w_out[l]
        x = x + rms_norm_2(mix, g_post_mix[l])
        h = rms_norm_2(x, g_pre_cross[l])
        mem_n = rms_norm_2(mem, g_mem[l])
        c = cross_attention(h, mem_n, w_cq[l], w_ckv[l], w_co[l])
        x = x + rms_norm_2(c, g_post_cross[l])
        h = rms_norm_2(x, g_pre_ffn[l])
        gu = h @ w_gate_up[l]
        f = (jax.nn.silu(gu[..., :D_FF]) * gu[..., D_FF:]) @ w_down[l]
        x = x + rms_norm_2(f, g_post_ffn[l])
    return x


def setup_inputs(seed=0):
    out = dict(first_inputs(seed))
    for name, value in second_inputs(seed + 1).items():
        if name != "x":
            out[name + "_2"] = value
    return out


def reference(
    x, norm1_gain, w_in, gla_up_fwd, gla_up_fwd_bias, gla_up_bwd, gla_up_bwd_bias, gla_out_gain,
    q_norm_gain, k_norm_gain, att_out_gain, w_out, norm2_gain, w_group, b_group, w_expert,
    b_expert, w_gate, w_up, w_down, final_gain, mem_2, g_pre_mix_2, w_in_2, w_out_2,
    g_post_mix_2, g_pre_cross_2, g_mem_2, w_cq_2, w_ckv_2, w_co_2, g_post_cross_2, g_pre_ffn_2,
    w_gate_up_2, w_down_2, g_post_ffn_2,
):
    x = first_block(
        x, norm1_gain, w_in, gla_up_fwd, gla_up_fwd_bias, gla_up_bwd, gla_up_bwd_bias,
        gla_out_gain, q_norm_gain, k_norm_gain, att_out_gain, w_out, norm2_gain, w_group,
        b_group, w_expert, b_expert, w_gate, w_up, w_down, final_gain,
    )
    return second_block(
        x, mem_2, g_pre_mix_2, w_in_2, w_out_2, g_post_mix_2, g_pre_cross_2, g_mem_2, w_cq_2,
        w_ckv_2, w_co_2, g_post_cross_2, g_pre_ffn_2, w_gate_up_2, w_down_2, g_post_ffn_2,
    )


_drawn_inputs = setup_inputs


def setup_inputs(seed=0):
    import zlib

    import numpy as np

    out = dict(_drawn_inputs(seed))
    spreads = {}
    factors = {'gla_up_fwd_bias': 2.936,
     'gla_out_gain': 3.78,
     'q_norm_gain': 2.859,
     'k_norm_gain': 2.768,
     'b_group': 4.863,
     'b_expert': 5.897,
     'att_out_gain': 4.025,
     'norm2_gain': 2.816}
    for name, (base, spread) in spreads.items():
        noise = np.random.default_rng([zlib.crc32(name.encode()), seed]).standard_normal(out[name].shape)
        drawn = base * np.exp(spread * noise) if base else spread * noise
        out[name] = __import__('jax').numpy.asarray(drawn.astype(out[name].dtype))
    for name, factor in factors.items():
        out[name] = (out[name] * factor).astype(out[name].dtype)
    return out
```

```python
from contextlib import ExitStack

import numpy as np

import concourse.bass as bass
from concourse import mybir

F32 = mybir.dt.float32
I32 = mybir.dt.int32
ALU = mybir.AluOpType
ACT = mybir.ActivationFunctionType
AX = mybir.AxisListType

P = 128
SEQ, D = 256, 1024
TT = SEQ // P
KD = D // P
EPS = 1e-6

GLA_H, GLA_DK, GLA_DV, GLA_CHUNK, GLA_RANK = 4, 64, 128, 64, 16
GATE_NORM = 16.0
GQA_H, GQA_KV, HD = 8, 2, 64
NG, EPG, NE, F_EXP = 8, 8, 64, 512
D_IN = 2336
C_GQ, C_GK, C_GV, C_GG, C_Z, C_AQ, C_AK, C_AV = 0, 256, 512, 1024, 1536, 1568, 2080, 2208

D_IN2 = 3072
C_MQ, C_MK, C_MV, C_RQ, C_RK, C_RV, C_RG = 0, 512, 1024, 1536, 1792, 2048, 2560
MOBA_H, RET_H, RET_DK, RET_DV = 8, 4, 64, 128
CROSS_H, CROSS_D = 4, 256
D_FF = 2816
KF = D_FF // P
GU_COLS = 256
N_GU = D_FF // GU_COLS

RING, SLOT = 6, 4096
TOK = 32
BATCH = 4
NB = NE // BATCH
MAX_ROUNDS = SEQ // TOK
NEG = -1e30

IN_UNITS = [(C, min(512, D_IN - C)) for C in (1536, 0, 512, 2048, 1024)]
OUT_UNITS = [(0, 512), (512, 512)]
PRE_UNITS = len(IN_UNITS) + len(OUT_UNITS)
MOE_UNITS = [("a", 0), ("b", 0), ("a", 1), ("b", 1), ("d", 0), ("a", 2), ("b", 2), ("d", 1), ("a", 3), ("b", 3),
             ("d", 2), ("d", 3)]
assert len(MOE_UNITS) == 2 * RING


def shape_constants():
    f = np.float32
    i = np.arange(P)
    s, t = i[:, None], i[None, :]
    same = (s // GLA_CHUNK) == (t // GLA_CHUNK)
    half = GLA_CHUNK // 2
    fwd = same & (s <= t)
    bwd = same & (s >= t)
    ref_f = same & (s % GLA_CHUNK <= half - 1)
    ref_b = same & (s % GLA_CHUNK >= half)
    cols = {
        "ident": np.eye(P, dtype=f),
        "cum_f": np.concatenate([fwd.astype(f) - ref_f, fwd], 1),
        "cum_b": np.concatenate([bwd.astype(f) - ref_b, bwd], 1),
        "rest_f": same & (s > t),
        "rest_b": same & (s < t),
        "before": s < t,
        "ones": np.ones((P, P)),
        "rank8": np.tile(NG - np.arange(NG), (P, 1)),
        "rank64": np.tile(NE - np.arange(NE), (P, 1)),
        "slot": np.tile(np.arange(TOK), (P, 1)),
        "neghalf": np.full((P, 32), -0.5),
        "rounds": np.tile(TOK * np.arange(1, MAX_ROUNDS), (P, 1)),
    }
    pos = np.arange(SEQ)
    inv = (f(10000.0) ** (-np.arange(0, 32, 2, dtype=f) / f(32))).astype(f)
    ang = np.concatenate([(pos // 64).astype(f)[:, None] * inv, (pos % 64).astype(f)[:, None] * inv], -1).astype(f)
    cos, sin = np.cos(ang).astype(f), np.sin(ang).astype(f)
    by_tile = lambda a: a.reshape(TT, P, -1).transpose(1, 0, 2).reshape(P, -1)
    cols["gqa_cos"] = by_tile(np.repeat(cos, 2, axis=1))
    cols["gqa_sin"] = by_tile(sin)
    cols["gqa_nsin"] = by_tile(-sin)
    at, n = {}, 0
    for name, a in cols.items():
        at[name] = (n, n + a.shape[1])
        n += a.shape[1]
    c1 = np.concatenate([np.asarray(a, f) for a in cols.values()], 1)

    causal = np.where(t <= s, 0.0, NEG)
    cols2 = {"causal": np.concatenate([np.zeros((P, P)), causal], 1)}
    inv_m = (f(500000.0) ** (-np.arange(8, dtype=f) * f(2.0) / f(16))).astype(f)
    am = (pos.astype(f)[:, None] * inv_m).astype(f)
    inv_r = (f(1.0) / (f(10000.0) ** np.linspace(0.0, 1.0, RET_DK // 2, dtype=f))).astype(f)
    ar = (pos.astype(f)[:, None] * inv_r).astype(f)
    cols2["moba_cos"], cols2["moba_sin"] = by_tile(np.cos(am).astype(f)), by_tile(np.sin(am).astype(f))
    cols2["ret_cos"], cols2["ret_sin"] = by_tile(np.cos(ar).astype(f)), by_tile(np.sin(ar).astype(f))
    q, k = np.arange(SEQ)[None, :], np.arange(SEQ)[:, None]
    dec = []
    for h in range(RET_H):
        log_g = np.log(1.0 - 2.0 ** (-5.0 - h))
        m = np.where(q >= k, np.exp(log_g * np.maximum(q - k, 0)), 0.0) * RET_DK ** -0.5
        dec += [m[:P, :], m[P:, P:]]
    cols2["decay"] = np.concatenate(dec, 1)
    at2, n = {}, 0
    for name, a in cols2.items():
        at2[name] = (n, n + a.shape[1])
        n += a.shape[1]
    c2 = np.concatenate([np.asarray(a, f) for a in cols2.values()], 1)

    mask = np.concatenate([fwd, fwd, bwd, bwd], 1).astype(np.int32)
    return c1, at, c2, at2, mask


def build(nc, t_in, consts, out):
    c1_at, c2_at = consts["c1_at"], consts["c2_at"]
    with ExitStack() as ctx:
        def sb(name, cols, dt=F32):
            return ctx.enter_context(nc.sbuf_tensor(name, [P, cols], dt))

        sems, counted = {}, {}
        for signal, per_stage, stages in (
                ("ss", 2, "n1 att mm n2 fin pm om pc oc pf of"),
                ("rstd", 1, "n1 gqa gla att mm n2 fin pm ret om pc oc pf of"),
                ("n", 2, "n1 mix mm n2 pm mix2 pc cmix pf"),
                ("tp", 4, "n1 mix mm n2 pm mix2 pc cmix pf"),
                ("Ta", 2, "n1 mix mm n2 pm mix2 pc cmix pf"),
                ("Tv", 2, "n1 mix mm n2 pm mix2 pc cmix pf")):
            for i, stage in enumerate(stages.split()):
                counted[f"{stage}_{signal}"] = ("all_" + signal, per_stage * i)
        for signal, counts in (("mm", (10, 4, 4, 4, 12, 4, 4, 4)), ("ev0", (5, 2, 2, 2, 6, 2, 2, 2)),
                               ("ev1", (5, 2, 2, 2, 6, 2, 2, 2))):
            base = 0
            for stage, n in zip("in out ck cv in2 out2 cq co".split(), counts):
                if (stage, signal) != ("out", "ev0"):
                    counted[f"{stage}_{signal}"] = ("all_" + signal, base)
                    base += n

        def S(name):
            name = counted.get(name, (name, 0))[0]
            if name not in sems:
                sems[name] = ctx.enter_context(nc.semaphore(name))
            return sems[name]

        def at(name, value):
            return S(name), counted.get(name, (name, 0))[1] + value

        ring = sb("ring", RING * SLOT)
        x = sb("x", TT * D).rearrange("p (t d) -> p t d", t=TT)
        xn = sb("xn", TT * D).rearrange("p (t d) -> p t d", t=TT)
        xT_ = sb("xT", KD * SEQ)
        xT = xT_.rearrange("p (k s) -> p k s", k=KD)
        mix_ = sb("mix", TT * D)
        mix = mix_.rearrange("p (t d) -> p t d", t=TT)
        big = sb("big", 6144)
        aux = sb("aux", 7680)
        c1 = sb("c1", consts["c1"].shape[1])
        c2 = sb("c2", consts["c2"].shape[1])
        gla_mask = sb("gla_mask", 4 * P, I32)
        row_gain = sb("row_gain", 2 * D).rearrange("p (r d) -> p r d", r=2)
        col_gain = sb("col_gain", 5 * KD).rearrange("p (r k) -> p r k", r=5)
        stat = sb("stat", 128)
        rounds_i = sb("rounds_i", 1, I32)

        def C1(name, lo=0, hi=None):
            a, b = c1_at[name]
            return c1[:, a + lo:(b if hi is None else a + hi)]

        def C2(name, lo=0, hi=None):
            a, b = c2_at[name]
            return c2[:, a + lo:(b if hi is None else a + hi)]

        ident = C1("ident")

        bank = [ctx.enter_context(nc.psum_tensor(f"bank{i}", [P, 512], F32)) for i in range(8)]

        KV_PLACE = {(0, 0): 0, (0, 2): 1, (1, 2): 2, (0, 1): 0, (1, 3): 1, (1, 1): 2}

        def kv_of(i4, ch):
            c = KV_PLACE[i4 // 2, ch]
            return bank[4 + i4 % 2 + 2 * (ch % 2)][:, c * P:(c + 1) * P]

        def slot(g):
            return ring[:, (g % RING) * SLOT:(g % RING + 1) * SLOT]

        proj = big[:, 0:TT * D_IN].rearrange("p (t c) -> p t c", t=TT)
        smallw = aux[:, 0:1024]
        la = aux[:, 0:1024].rearrange("p (t c) -> p t c", t=TT)
        decay_exp = aux[:, 1024:3072].rearrange("p (i t w c) -> p i t w c", i=4, t=TT, w=2)
        key_exp = aux[:, 3072:4096].rearrange("p (i t c) -> p i t c", i=4, t=TT)
        gqT = aux[:, 4096:4608].rearrange("p (r s) -> p r s", r=2)
        gkT = aux[:, 4608:5120].rearrange("p (r s) -> p r s", r=2)
        key_rest = aux[:, 5120:6144].rearrange("p (i t c) -> p i t c", i=2, t=TT)
        state = aux[:, 6144:7680].rearrange("p (i n c) -> p i n c", i=4, n=3)
        scores = xT_[:, :].rearrange("p (h c) -> p h c", h=GLA_H)
        o_gla = la
        gate_tmp = mix_[:, :].rearrange("p (n t c) -> p n t c", n=2, t=TT)
        small = big[:, TT * D_IN:6144]
        zT = small[:, 0:SEQ]
        gate_up = small[:, 256:768]
        chunk_decay = sb("chunk_decay", 16).rearrange("p (i n) -> p i n", i=4)
        gla_gain = sb("gla_gain", GLA_DV)[:, :]
        qk_gain = small[:, 768:896]
        att_gain = small[:, 896:1408]
        gqa_tmp = xn[:, :, :].rearrange("p t d -> p (t d)")[:, 0:1280].rearrange("p (t h d) -> p t h d", t=TT, d=HD)
        kdup = xn[:, :, :].rearrange("p t d -> p (t d)")[:, 1280:1792].rearrange("p (t k u d) -> p t k u d", t=TT, k=2, u=2)
        gqa_qT = aux[:, 1024:2048].rearrange("p (r s) -> p r s", r=4)
        gqa_kT = aux[:, 2048:2560].rearrange("p (r s) -> p r s", r=2)
        probs = aux[:, 5120:5632].rearrange("p (i c) -> p i c", i=2)
        probsT = aux[:, 5632:6144].rearrange("p (i c) -> p i c", i=2)
        o_att = aux[:, 3072:4096].rearrange("p (t c) -> p t c", t=TT)
        negmax = stat[:, 64:80]
        esum = stat[:, 80:96]
        ersum = stat[:, 96:112]

        cut_at = [0]

        def cut(n):
            cut_at[0] += n
            return big[:, cut_at[0] - n:cut_at[0]]

        w_route = aux[:, 6144:6144 + KD * 72].rearrange("p (k e) -> p k e", k=KD)
        b_route = aux[0:1, 6720:6792]
        logits = cut(2 * 72).rearrange("p (t e) -> p t e", t=TT)
        rt = [cut(128).rearrange("p (t e) -> p t e", t=TT) for _ in range(5)]
        rg = [cut(16).rearrange("p (t e) -> p t e", t=TT) for _ in range(4)]
        rs = [cut(TT) for _ in range(12)]
        picked = cut(2 * NE).rearrange("p (t e) -> p t e", t=TT)
        gate_of = cut(2 * NE).rearrange("p (t e) -> p t e", t=TT)
        place = cut(2 * NE).rearrange("p (t e) -> p t e", t=TT)
        slots_now = cut(TOK)
        rounds_f = cut(8)
        sel = cut(2 * P).rearrange("p (t s) -> p t s", t=TT)
        sel_gate = cut(2 * P).rearrange("p (t s) -> p t s", t=TT)
        sel_gateT = cut(2 * P)
        xg = cut(KD * P).rearrange("p (k s) -> p k s", k=KD)
        eg = cut(2 * P).rearrange("p (i c) -> p i c", i=2)
        hx = cut(2 * P).rearrange("p (i c) -> p i c", i=2)
        hr = cut(P)
        hT = cut(2 * P).rearrange("p (i c) -> p i c", i=2)
        y_batch = cut(D)
        assert cut_at[0] <= 6144

        proj2 = big[:, :].rearrange("p (t c) -> p t c", t=TT)
        xn_flat = xn[:, :, :].rearrange("p t d -> p (t d)")
        c_kT = aux[:, 0:2048].rearrange("p (k s) -> p k s", k=KD)
        c_v = aux[:, 4096:6144].rearrange("p (t d) -> p t d", t=TT)
        mem = aux[:, 0:2048].rearrange("p (t d) -> p t d", t=TT)
        memT = aux[:, 2048:4096].rearrange("p (k s) -> p k s", k=KD)
        m_qT = xT_[:, 0:1024].rearrange("p (r s) -> p r s", r=4)
        m_kT = xT_[:, 1024:2048].rearrange("p (r s) -> p r s", r=4)
        r_qT = aux[:, 2048:2560].rearrange("p (r s) -> p r s", r=2)
        r_kT = aux[:, 2560:3072].rearrange("p (r s) -> p r s", r=2)
        probs2 = aux[:, 3072:3584].rearrange("p (i c) -> p i c", i=2)
        probsT2 = aux[:, 3584:4096].rearrange("p (i c) -> p i c", i=2)
        r_scores = aux[:, 6144:7680].rearrange("p (h c) -> p h c", h=RET_H)
        r_square = aux[:, 6144:7168].rearrange("p (t c) -> p t c", t=TT)
        rope_tmp = xn_flat.rearrange("p (n t c) -> p n t c", n=4, t=TT)
        ret_o = xn_flat[:, 0:1024].rearrange("p (t c) -> p t c", t=TT)
        ret_g = xn_flat[:, 1024:2048].rearrange("p (t c) -> p t c", t=TT)
        y = mix
        c_qT = big[:, 0:2048].rearrange("p (k s) -> p k s", k=KD)
        ffT = big[:, 0:KF * SEQ].rearrange("p (k s) -> p k s", k=KF)
        ff_e = xn_flat[:, 0:1024].rearrange("p (i c) -> p i c", i=4)

        x_rows = t_in["x"][0].rearrange("(t p) d -> p t d", p=P)
        mem_rows = t_in["mem_2"][0].rearrange("(t p) d -> p t d", p=P)
        out_rows = out[0].rearrange("(t p) d -> p t d", p=P)

        def chunks(w):
            return w.rearrange("(k p) c -> p k c", p=P)

        used = {g: ("in_mm", 2 * g + 2) for g in range(len(IN_UNITS))}
        for u in range(len(OUT_UNITS)):
            used[len(IN_UNITS) + u] = ("out_mm", 2 * u + 2)
        G2 = PRE_UNITS + len(MOE_UNITS)
        post = []

        def cols_unit(w, c, signal, value):
            post.append((chunks(w)[:, :, c:c + 512], lambda s: s.rearrange("p (k c) -> p k c", k=KD), signal, value))

        for u in range(4):
            cols_unit(t_in["w_ckv_2"][0], 512 * u, "ck_mm" if u < 2 else "cv_mm", 2 * (u % 2) + 2)
        for u in range(6):
            cols_unit(t_in["w_in_2"][0], 512 * u, "in2_mm", 2 * u + 2)
        for u in range(2):
            cols_unit(t_in["w_out_2"][0], 512 * u, "out2_mm", 2 * u + 2)
        for u in range(2):
            cols_unit(t_in["w_cq_2"][0], 512 * u, "cq_mm", 2 * u + 2)
        for u in range(2):
            cols_unit(t_in["w_co_2"][0], 512 * u, "co_mm", 2 * u + 2)
        for u in range(N_GU):
            w = t_in["w_gate_up_2"][0]
            post.append(((chunks(w)[:, :, GU_COLS * u:GU_COLS * (u + 1)],
                          chunks(w)[:, :, D_FF + GU_COLS * u:D_FF + GU_COLS * (u + 1)]),
                         lambda s: s.rearrange("p (k w c) -> p k w c", k=KD, w=2), "gu_mm", 2 * u + 2))
        FF_PARTS = [(0, 8), (8, 16), (16, 22)]
        for half in range(2):
            for n, (k0, k1) in enumerate(FF_PARTS):
                post.append((chunks(t_in["w_down_2"][0])[:, k0:k1, 512 * half:512 * half + 512],
                             lambda s, m=k1 - k0: s[:, 0:512 * m].rearrange("p (k c) -> p k c", k=m),
                             "down_mm", 3 * half + n + 1))

        def post_wait(eng, u):
            eng.wait_ge(*at(f"w2_in{u % RING}", 32 * (u // RING + 1)))

        block = ctx.enter_context(nc.Block())

        @block.sync
        def _(sp):
            sp.dma_start(x[:, :, :], x_rows).then_inc(S("x_in"), 16)
            for g in range(PRE_UNITS):
                if g >= RING:
                    sp.wait_ge(*at(used[g - RING][0], used[g - RING][1]))
                if g < len(IN_UNITS):
                    c, n = IN_UNITS[g]
                    src = chunks(t_in["w_in"][0])[:, :, c:c + n]
                    dst = slot(g)[:, 0:KD * n].rearrange("p (k c) -> p k c", k=KD)
                else:
                    c, n = OUT_UNITS[g - len(IN_UNITS)]
                    src = chunks(t_in["w_out"][0])[:, :, c:c + n]
                    dst = slot(g).rearrange("p (k c) -> p k c", k=KD)
                sp.dma_start(dst, src).then_inc(S(f"w1_in{g % RING}"), 16)

            def moe_load(u, expert):
                part, _ = MOE_UNITS[u]
                dst, arrived = slot(PRE_UNITS + u), S(f"moe_in{u % RING}")
                if part == "d":
                    w = t_in["w_down"][0, expert].rearrange("e (k p) c -> p (e k) c", p=P)
                    v = dst.rearrange("p (k c) -> p k c", k=4)
                    sp.dma_start(v[:, 2:4, :], w[:, 2:4, :]).then_inc(arrived, 16)
                    sp.dma_start(v[:, 0:2, :], w[:, 0:2, :]).then_inc(arrived, 16)
                else:
                    k0 = 0 if part == "a" else 4
                    v = dst.rearrange("p (k w c) -> p k w c", k=4, w=2)
                    for n, name in enumerate(("w_gate", "w_up")):
                        w = t_in[name][0, expert].rearrange("e (k p) c -> p (e k) c", p=P)
                        sp.dma_start(v[:, :, n, :], w[:, k0:k0 + 4, :]).then_inc(arrived, 16)

            def moe_slot_free(u, done):
                part, q = MOE_UNITS[u - RING]
                n = done + q + 1 if u >= RING else done - BATCH + q + 1
                sp.wait_ge(*at({"a": "moe_a_used", "b": "moe_gu", "d": "moe_d"}[part], n))

            def experts_of(b, u):
                return bass.ds(b * BATCH + MOE_UNITS[u][1], 1)

            for u in range(RING):
                sp.wait_ge(*at(used[PRE_UNITS + u - RING][0], used[PRE_UNITS + u - RING][1]))
                moe_load(u, bass.ds(MOE_UNITS[u][1], 1))
            with sp.Fori(0, NB - 1) as b:
                for u in range(RING, 2 * RING):
                    moe_slot_free(u, b * BATCH)
                    moe_load(u, experts_of(b, u))
                for u in range(RING):
                    moe_slot_free(u, b * BATCH + BATCH)
                    moe_load(u, experts_of(b + 1, u))
            for u in range(RING, 2 * RING):
                moe_slot_free(u, (NB - 1) * BATCH)
                moe_load(u, experts_of(NB - 1, u))
            sp.wait_ge(*at("rounds_ready", 1))
            rounds = sp.value_load(rounds_i[0:1, 0:1], min_val=1, max_val=MAX_ROUNDS)
            with sp.If(rounds > 1):
                with sp.Fori(1, rounds) as c, sp.Fori(0, NB) as b:
                    for u in range(2 * RING):
                        moe_slot_free(u, c * NE + b * BATCH)
                        moe_load(u, experts_of(b, u))

            for u, (src, view, signal, value) in enumerate(post):
                if u < RING:
                    sp.wait_ge(*at("moe_gu" if u < 4 else "moe_d", rounds * NE))
                else:
                    sp.wait_ge(*at(post[u - RING][2], post[u - RING][3]))
                dst = view(slot(G2 + u))
                if isinstance(src, tuple):
                    for w in range(2):
                        sp.dma_start(dst[:, :, w, :], src[w]).then_inc(S(f"w2_in{u % RING}"), 16)
                else:
                    h = src.shape[1] // 2
                    sp.dma_start(dst[:, 0:h, :], src[:, 0:h, :]).then_inc(S(f"w2_in{u % RING}"), 16)
                    sp.dma_start(dst[:, h:, :], src[:, h:, :]).then_inc(S(f"w2_in{u % RING}"), 16)
            for t in range(TT):
                sp.wait_ge(*at("ffn_x", t + 1))
                sp.dma_start(out_rows[:, t, :], x[:, t, :]).then_inc(S("stored"), 16)
            sp.wait_ge(*at("stored", 16 * TT))

        @block.gpsimd
        def _(pool):
            def load(dst, src, name):
                pool.dma_start(dst, src).then_inc(S(name), 16)

            load(c1[:, :], consts["c1"], "c1_in")
            for r, name in enumerate(("norm1_gain", "g_pre_mix_2", "g_mem_2", "g_pre_cross_2", "g_pre_ffn_2")):
                with nc.allow_non_contiguous_dma(reason="gains as columns, 4 KB"):
                    load(col_gain[:, r, :], t_in[name][0].rearrange("(k p) -> p k", p=P), "colgain_in")
            pool.memset(gate_up[0:33, :], 0.0).then_inc(S("gateup_zero"), 1)
            pool.memset(zT[0:33, :], 1.0).then_inc(S("zT_one"), 1)
            pool.wait_ge(*at("gateup_zero", 1))
            W = GLA_H * GLA_DK
            load(gate_up[0:16, 0:W], t_in["gla_up_fwd"][0], "gateup_in")
            load(gate_up[16:32, W:2 * W], t_in["gla_up_bwd"][0], "gateup_in")
            load(gate_up[32:33, 0:W], t_in["gla_up_fwd_bias"], "gateup_in")
            load(gate_up[32:33, W:2 * W], t_in["gla_up_bwd_bias"], "gateup_in")
            load(gla_mask[:, :], consts["mask"], "mask_in")
            load(gla_gain, t_in["gla_out_gain"][0:1, :].to_broadcast([P, GLA_DV]), "glagain_in")
            load(qk_gain[:, 0:HD], t_in["q_norm_gain"][0:1, :].to_broadcast([P, HD]), "qkgain_in")
            load(qk_gain[:, HD:], t_in["k_norm_gain"][0:1, :].to_broadcast([P, HD]), "qkgain_in")
            load(att_gain, t_in["att_out_gain"][0:1, :].to_broadcast([P, 512]), "attgain_in")
            load(row_gain[:, 0, :], t_in["norm2_gain"][0:1, :].to_broadcast([P, D]), "norm2gain_in")
            load(row_gain[:, 1, :], t_in["final_gain"].rearrange("(o d) -> o d", o=1).to_broadcast([P, D]), "finalgain_in")
            load(c2[:, :], consts["c2"], "c2_in")
            pool_chain = [0]

            def rstd(name, n, width, col, ready):
                pool.wait_ge(*at(f"{name}_ss", ready))
                pool.tensor_scalar(stat[:, col:col + n], stat[:, col:col + n], 1.0 / width, EPS, ALU.mult,
                                   ALU.add).then_inc(S("pool_chain"), 1)
                pool_chain[0] += 1
                pool.wait_ge(*at("pool_chain", pool_chain[0]))
                pool.tensor_tensor(stat[:, col:col + n], stat[:, col:col + n], C1("neghalf", 0, n),
                                   ALU.pow).then_inc(S(f"{name}_rstd"), 1)

            pool.wait_ge(*at("c1_in", 16))
            rstd("n1", 2, D, 0, 2)
            pool.wait_ge(*at("in_mm", 2 * len(IN_UNITS)))
            pool.memset(xT_[:, :], 0.0).then_inc(S("scores_zero"), 1)
            rstd("gqa", 2 * (GQA_H + GQA_KV), HD, 16, 1)
            rstd("gla", 2 * GLA_H, GLA_DV, 8, 1)
            rstd("att", 2, 512, 2, 2)
            pool.wait_ge(*at("gla_o", TT))
            with nc.allow_non_contiguous_dma(reason="router weights, 72 columns"):
                load(w_route[:, :, 0:NG], chunks(t_in["w_group"][0]), "route_in")
                load(w_route[:, :, NG:], chunks(t_in["w_expert"][0]), "route_in")
            load(b_route[:, 0:NG], t_in["b_group"], "route_in")
            load(b_route[:, NG:], t_in["b_expert"], "route_in")
            pool.wait_ge(*at("mix_n", TT))
            load(mem, mem_rows, "mem_in")
            rstd("mm", 2, D, 36, 2)
            rstd("n2", 2, D, 4, 2)
            rstd("fin", 2, D, 6, 2)
            load(row_gain[:, 0, :], t_in["g_post_mix_2"][0:1, :].to_broadcast([P, D]), "postmix_in")
            rstd("pm", 2, D, 38, 2)
            pool.wait_ge(*at("x_final", TT))
            load(row_gain[:, 1, :], t_in["g_post_cross_2"][0:1, :].to_broadcast([P, D]), "postcross_in")
            rstd("ret", 2 * RET_H, RET_DV, 40, 1)
            rstd("om", 2, D, 48, 2)
            rstd("pc", 2, D, 50, 2)
            pool.wait_ge(*at("om_x", TT))
            load(row_gain[:, 0, :], t_in["g_post_ffn_2"][0:1, :].to_broadcast([P, D]), "postffn_in")
            rstd("oc", 2, D, 52, 2)
            rstd("pf", 2, D, 54, 2)
            rstd("of", 2, D, 56, 2)

        @block.tensor
        def _(pe):
            def transposes(name, src, n_src, k_total=KD):
                for kp in range(k_total // 2):
                    b = bank[4 + kp % 2]
                    if kp >= 2:
                        pe.wait_ge(*at(f"{name}_T{'av'[kp % 2]}", kp // 2))
                    for t in range(TT):
                        if kp == 0:
                            pe.wait_ge(*at(f"{name}_n", n_src[t]))
                        for kk in range(2):
                            k = 2 * kp + kk
                            i = pe.transpose(b[:, kk * SEQ + t * P:kk * SEQ + t * P + P], src[:, t, k * P:(k + 1) * P],
                                             ident)
                    i.then_inc(S(f"{name}_tp"), 1)

            def wait_T(name, k_total=KD):
                pe.wait_ge(*at(f"{name}_Ta", k_total // 4))
                pe.wait_ge(*at(f"{name}_Tv", k_total // 4))

            def linear(name, lhsT, u, w, n=512, kd=KD):
                for t in range(TT):
                    j = 2 * u + t
                    if j >= 4:
                        pe.wait_ge(*at(f"{name}_ev{t}", (j - 4) // 2 + 1))
                    for k in range(kd):
                        i = pe.matmul(bank[j % 4][:, 0:n], lhsT[:, k, t * P:(t + 1) * P], w[:, k, :],
                                      start=(k == 0), stop=(k == kd - 1))
                    i.then_inc(S(f"{name}_mm"), 1)

            def attention(pe, name, units, qk, v_of, dv, pr, prT, key_tiles):
                heads = units // TT
                order = [(t, h) for t in range(TT) for h in range(heads)]
                for n in range(units + 2):
                    if n < units:
                        t, h = order[n]
                        if n >= 2:
                            pe.wait_ge(*at(f"{name}_exp", n - 1))
                        parts = qk(h, t)
                        parts = parts if isinstance(parts, list) else [parts]
                        w = key_tiles(t) * P
                        for m, (a, b) in enumerate(parts):
                            i = pe.matmul(bank[2 + n % 2][:, 0:w], a, b[:, 0:w], start=(m == 0), stop=(m == len(parts) - 1))
                        i.then_inc(S(f"{name}_sc"), 1)
                    if 1 <= n <= units:
                        m = n - 1
                        pe.wait_ge(*at(f"{name}_exp", m + 1))
                        if m >= 2:
                            pe.wait_ge(*at(f"{name}_PT", m - 1))
                        for k in range(key_tiles(order[m][0])):
                            i = pe.transpose(bank[6 + m % 2][:, k * P:(k + 1) * P], pr[:, m % 2, k * P:(k + 1) * P], ident)
                        i.then_inc(S(f"{name}_ptp"), 1)
                    if n >= 2:
                        m = n - 2
                        t, h = order[m]
                        pe.wait_ge(*at(f"{name}_PT", m + 1))
                        kt = key_tiles(t)
                        per = 512 // dv
                        b, c = (4 + t, h) if heads <= per else (None, None)
                        if heads > per:
                            b, c = (4 if t == 0 else 0) + h // per, h % per
                        for k in range(kt):
                            i = pe.matmul(bank[b][:, c * dv:(c + 1) * dv], prT[:, m % 2, k * P:(k + 1) * P], v_of(h, t, k),
                                          start=(k == 0), stop=(k == kt - 1))
                        i.then_inc(S(f"{name}_pv"), 1)

            pe.wait_ge(*at("c1_in", 16))
            transposes("n1", xn, (1, 2))
            wait_T("n1")
            for u, (c, n) in enumerate(IN_UNITS):
                pe.wait_ge(*at(f"w1_in{u}", 16))
                linear("in", xT, u, slot(u)[:, 0:KD * n].rearrange("p (k c) -> p k c", k=KD), n)
                if u == 1:
                    for t in range(TT):
                        pe.wait_ge(*at(f"in_ev{t}", 1))
                    for t in range(TT):
                        i = pe.transpose(bank[4][0:32, t * P:(t + 1) * P], proj[:, t, C_Z:C_Z + 32], ident)
                    i.then_inc(S("zT_tp"), 1)
                if u == 2:
                    pe.wait_ge(*at("zT_ev", 1))
                    pe.wait_ge(*at("gateup_in", 64))
                    for t in range(TT):
                        pe.matmul(bank[6 + t][:, :], zT[0:33, t * P:(t + 1) * P], gate_up[0:33, :], start=True,
                                  stop=True).then_inc(S("gate_mm"), 1)
                if u == 3:
                    for t in range(TT):
                        pe.wait_ge(*at(f"in_ev{t}", 2))
                    for w, c0 in enumerate((C_GQ, C_GK)):
                        for r in range(2):
                            for t in range(TT):
                                i = pe.transpose(bank[4 + w][:, r * SEQ + t * P:r * SEQ + (t + 1) * P],
                                                 proj[:, t, c0 + r * P:c0 + (r + 1) * P], ident)
                        i.then_inc(S("gqk_tp"), 1)
            for i4 in range(4):
                di, r = i4 // 2, i4 % 2
                if i4 == 0:
                    pe.wait_ge(*at("la", 2))
                    pe.wait_ge(*at("gqkT", 2))
                if i4 >= 2:
                    pe.wait_ge(*at("sum_exp", i4 - 1))
                for t in range(TT):
                    i = pe.matmul(bank[4 + i4 % 2][:, t * SEQ:(t + 1) * SEQ],
                                  la[:, t, di * SEQ + r * P:di * SEQ + (r + 1) * P],
                                  C1("cum_f" if di == 0 else "cum_b"), start=True, stop=True)
                i.then_inc(S("sum_mm"), 1)
            for di in range(2):
                for t in range(TT):
                    i = pe.matmul(bank[6 + di][:, t * SEQ:(t + 1) * SEQ], C1("rest_f" if di == 0 else "rest_b"),
                                  la[:, t, di * SEQ:(di + 1) * SEQ], start=True, stop=True)
                i.then_inc(S("rest_mm"), 1)
            for h in range(GLA_H):
                r, o = h // 2, 64 * (h % 2)
                if h == 0:
                    for t in range(TT):
                        pe.wait_ge(*at(f"in_ev{t}", len(IN_UNITS)))
                for di in range(2):
                    pe.wait_ge(*at("gla_qk", 2 * di + r + 1))
                    for t in range(TT):
                        i = pe.matmul(bank[h][:, (2 * di + t) * P:(2 * di + t + 1) * P],
                                      key_exp[o:o + 64, 2 * di + r, t, :], decay_exp[o:o + 64, 2 * di + r, t, 0, :],
                                      start=True, stop=True)
                i.then_inc(S("gla_sc"), 1)
            for i4 in range(4):
                di, r = i4 // 2, i4 % 2
                pe.wait_ge(*at("key_rest", di + 1))
                if i4 == 0:
                    pe.wait_ge(*at("sum_exp", 4))
                    pe.wait_ge(*at("key_rest", 2))
                for n in range(3):
                    ch = n if di == 0 else 3 - n
                    t, o = ch // 2, 64 * (ch % 2)
                    for hh in range(2):
                        i = pe.matmul(kv_of(i4, ch)[64 * hh:64 * hh + 64, :],
                                      key_rest[o:o + 64, di, t, r * P + 64 * hh:r * P + 64 * hh + 64],
                                      proj[o:o + 64, t, C_GV + (2 * r + hh) * P:C_GV + (2 * r + hh + 1) * P],
                                      start=True, stop=True)
                i.then_inc(S("gla_kv"), 1)
            pe.wait_ge(*at("gla_masked", GLA_H))
            pe.wait_ge(*at("gla_state", 4))
            for t in range(TT):
                for h in range(GLA_H):
                    r, o = h // 2, 64 * (h % 2)
                    b = bank[2 * (h % 2) + t]
                    dst = b[:, r * P:(r + 1) * P]
                    for di in range(2):
                        pe.matmul(dst, scores[:, h, (2 * di + t) * P:(2 * di + t + 1) * P],
                                  proj[:, t, C_GV + h * P:C_GV + (h + 1) * P], start=(di == 0), stop=(di == 1))
                    parts = [(di, ch) for ch in (2 * t, 2 * t + 1) for di in range(2)
                             if (ch > 0 if di == 0 else ch < 3)]
                    for di, ch in parts:
                        cc = 64 * (ch % 2)
                        n = ch - 1 if di == 0 else 2 - ch
                        i = pe.matmul(b[cc:cc + 64, r * P:(r + 1) * P],
                                      decay_exp[o:o + 64, 2 * di + r, t, 1, cc:cc + 64],
                                      state[o:o + 64, 2 * di + r, n, :], start=False, stop=True,
                                      skip_group_check=True)
                i.then_inc(S("gla_o"), 1)
            pe.wait_ge(*at("gqa_qk", 1))
            for t in range(TT):
                for r in range(4):
                    i = pe.transpose(bank[4 + r // 2][:, (r % 2) * SEQ + t * P:(r % 2) * SEQ + (t + 1) * P],
                                     proj[:, t, C_AQ + r * P:C_AQ + (r + 1) * P], ident)
            for t in range(TT):
                for r in range(2):
                    i = pe.transpose(bank[6][:, r * SEQ + t * P:r * SEQ + (t + 1) * P],
                                     kdup[:, t, r, :, :].rearrange("p u d -> p (u d)"), ident)
            i.then_inc(S("gqa_tp"), 1)
            pe.wait_ge(*at("gqa_T", 3))
            attention(pe, "gqa", 16, lambda h, t: (gqa_qT[64 * (h % 2):64 * (h % 2) + 64, h // 2, t * P:(t + 1) * P],
                                                   gqa_kT[64 * (h % 2):64 * (h % 2) + 64, h // 4, :]),
                      lambda h, t, k: proj[:, k, C_AV + (h // 4) * HD:C_AV + (h // 4 + 1) * HD], HD,
                      probs, probsT, lambda t: TT)
            transposes("mix", mix, (1, 2))
            wait_T("mix")
            for u in range(2):
                g = len(IN_UNITS) + u
                pe.wait_ge(*at(f"w1_in{g % RING}", 16 * (g // RING + 1)))
                linear("out", xT, u, slot(g).rearrange("p (k c) -> p k c", k=KD))
                if u == 0:
                    transposes("mm", mem, (1, 2))
            transposes("n2", xn, (1, 2))
            wait_T("n2")
            pe.wait_ge(*at("route_in", 64))
            for t in range(TT):
                pe.matmul(bank[t][:, 0:72], C1("ones")[0:1, :], b_route, start=True, stop=False)
                for k in range(KD):
                    i = pe.matmul(bank[t][:, 0:72], xT[:, k, t * P:(t + 1) * P], w_route[:, k, :], start=False,
                                  stop=(k == KD - 1))
            i.then_inc(S("route_mm"), 1)
            pe.wait_ge(*at("picked", 1))
            pe.matmul(bank[2][:, 0:NE], C1("before"), picked[:, 0, :], start=True, stop=True)
            pe.matmul(bank[2][:, NE:2 * NE], C1("before"), picked[:, 1, :], start=True, stop=False)
            pe.matmul(bank[2][:, NE:2 * NE], C1("ones"), picked[:, 0, :], start=False, stop=True)
            pe.matmul(bank[2][:, 2 * NE:3 * NE], C1("ones"), picked[:, 0, :], start=True, stop=False)
            pe.matmul(bank[2][:, 2 * NE:3 * NE], C1("ones"), picked[:, 1, :], start=False, stop=True
                      ).then_inc(S("place_mm"), 1)

            pe.wait_ge(*at("rounds_ready", 1))
            rounds = pe.value_load(rounds_i[0:1, 0:1], min_val=1, max_val=MAX_ROUNDS)
            with pe.Fori(0, rounds) as c, pe.Fori(0, NB) as b:
                it = c * NB + b

                def arrive(part, q):
                    u = MOE_UNITS.index((part, q))
                    pe.wait_ge(*at(f"moe_in{u % RING}", it * 64 + 32 * (u // RING + 1)))
                    return slot(PRE_UNITS + u)

                def gate_up_half(part, q):
                    w = arrive(part, q).rearrange("p (k w c) -> p k w c", k=4, w=2)
                    for k in range(4):
                        for j in range(4):
                            i = pe.matmul(bank[q % 2][TOK * j:TOK * (j + 1), 0:SEQ],
                                          xg[:, k + (0 if part == "a" else 4), TOK * q:TOK * (q + 1)],
                                          w[:, k, :, j * P:(j + 1) * P], start=(part == "a" and k == 0),
                                          stop=(part == "b" and k == 3), tile_position=(0, TOK * j))
                    i.then_inc(S("moe_a_used" if part == "a" else "moe_gu"), 1)

                def h_transpose(q):
                    pe.wait_ge(*at("moe_h", it * BATCH + q + 1))
                    pe.transpose(bank[4][:, 0:P], hx[:, q % 2, :], ident).then_inc(S("moe_hT_tp"), 1)

                def down(q):
                    w = arrive("d", q).rearrange("p (k c) -> p k c", k=4)
                    pe.wait_ge(*at("moe_hT", it * BATCH + q + 1))
                    for half in range(2):
                        for j in range(4):
                            i = pe.matmul(bank[6 + half][TOK * q:TOK * (q + 1), :], hT[:, q % 2, TOK * j:TOK * (j + 1)],
                                          w[:, j, half * 512:(half + 1) * 512], start=(j == 0), stop=(j == 3),
                                          tile_position=(0, TOK * q))
                    i.then_inc(S("moe_d"), 1)

                pe.wait_ge(*at("moe_sel", it + 1))
                for t in range(TT):
                    i = pe.transpose(bank[5][:, t * P:(t + 1) * P], sel_gate[:, t, :], ident)
                i.then_inc(S("moe_selT_tp"), 1)
                pe.wait_ge(*at("moe_xadd", it * 4 + 1))
                for k in range(KD):
                    for t in range(TT):
                        i = pe.matmul(bank[2 + k // 4][:, (k % 4) * P:(k % 4 + 1) * P], xn[:, t, k * P:(k + 1) * P],
                                      sel[:, t, :], start=(t == 0), stop=(t == TT - 1))
                    if k % 4 == 3:
                        i.then_inc(S("moe_xg_mm"), 1)
                pe.wait_ge(*at("moe_xg_a", it + 1))
                pe.wait_ge(*at("moe_xg_v", it + 1))
                gate_up_half("a", 0)
                gate_up_half("b", 0)
                for q in range(1, BATCH):
                    gate_up_half("a", q)
                    h_transpose(q - 1)
                    gate_up_half("b", q)
                    down(q - 1)
                h_transpose(BATCH - 1)
                down(BATCH - 1)
                pe.wait_ge(*at("moe_selT", it + 1))
                for half in range(2):
                    pe.wait_ge(*at("moe_y_a" if half == 0 else "moe_y_v", it + 1))
                    for t in range(TT):
                        n = 2 * half + t
                        if n >= 2:
                            pe.wait_ge(*at("moe_xadd", it * 4 + n))
                        pe.matmul(bank[2 + n % 2][:, :], sel_gateT[:, t * P:(t + 1) * P],
                                  y_batch[:, half * 512:(half + 1) * 512], start=True, stop=True
                                  ).then_inc(S("moe_cmb"), 1)
            def linear_T(name, u, rhsT, j0=0):
                w = slot(G2 + u).rearrange("p (k c) -> p k c", k=KD)
                for jj in range(2):
                    for m in range(2):
                        for k in range(KD):
                            i = pe.matmul(bank[j0 + jj][:, m * SEQ:(m + 1) * SEQ],
                                          w[:, k, (2 * jj + m) * P:(2 * jj + m + 1) * P], rhsT[:, k, :],
                                          start=(k == 0), stop=(k == KD - 1))
                    i.then_inc(S(f"{name}_mm"), 1)

            def post_linear(name, lhsT, u, g):
                post_wait(pe, g)
                linear(name, lhsT, u, slot(G2 + g).rearrange("p (k c) -> p k c", k=KD))

            def emptied(name, n):
                for t in range(TT):
                    pe.wait_ge(*at(f"{name}_ev{t}", n))

            wait_T("mm")
            pe.wait_ge(*at("moe_x", 1))
            for u in range(2):
                post_wait(pe, u)
                linear_T("ck", u, memT, 2 * u)
            emptied("ck", 2)
            for u in range(2):
                post_linear("cv", memT, u, 2 + u)
            transposes("pm", xn, (1, 2))
            wait_T("pm")
            emptied("cv", 2)
            for u in range(6):
                post_linear("in2", xT, u, 4 + u)
            emptied("in2", 6)
            pe.wait_ge(*at("rope", 1))
            for w, c0 in enumerate((C_MQ, C_MK)):
                for r in range(4):
                    for t in range(TT):
                        i = pe.transpose(bank[4 + 2 * w + r // 2][:, (r % 2) * SEQ + t * P:(r % 2) * SEQ + (t + 1) * P],
                                         proj2[:, t, c0 + r * P:c0 + (r + 1) * P], ident)
                    if r % 2 == 1:
                        i.then_inc(S("m_tp"), 1)
            pe.wait_ge(*at("rope", 2))
            for w, c0 in enumerate((C_RQ, C_RK)):
                for r in range(2):
                    for t in range(TT):
                        i = pe.transpose(bank[w][:, r * SEQ + t * P:r * SEQ + (t + 1) * P],
                                         proj2[:, t, c0 + r * P:c0 + (r + 1) * P], ident)
                i.then_inc(S("r_tp"), 1)
            pe.wait_ge(*at("r_T", 2))
            for h in range(RET_H):
                r, o = h // 2, 64 * (h % 2)
                pe.matmul(bank[h][:, 0:SEQ], r_kT[o:o + 64, r, 0:P], r_qT[o:o + 64, r, :], start=True, stop=True)
                pe.matmul(bank[h][:, SEQ:SEQ + P], r_kT[o:o + 64, r, P:SEQ], r_qT[o:o + 64, r, P:SEQ], start=True,
                          stop=True).then_inc(S("ret_sc"), 1)
            pe.wait_ge(*at("ret_decayed", RET_H))
            for t in range(TT):
                for h in range(RET_H):
                    for k in range(t + 1):
                        c = t * P if k == 0 else SEQ
                        i = pe.matmul(bank[t][:, h * P:(h + 1) * P], r_scores[:, h, c:c + P],
                                      proj2[:, k, C_RV + h * P:C_RV + (h + 1) * P], start=(k == 0), stop=(k == t))
                i.then_inc(S("ret_o"), 1)
            pe.wait_ge(*at("m_T", 4))
            attention(pe, "moba", 16, lambda h, t: (m_qT[64 * (h % 2):64 * (h % 2) + 64, h // 2, t * P:(t + 1) * P],
                                                    m_kT[64 * (h % 2):64 * (h % 2) + 64, h // 2, :]),
                      lambda h, t, k: proj2[:, k, C_MV + h * HD:C_MV + (h + 1) * HD], HD, probs2, probsT2,
                      lambda t: t + 1)
            transposes("mix2", mix, (1, 2))
            wait_T("mix2")
            for u in range(2):
                post_linear("out2", xT, u, 10 + u)
            transposes("pc", xn, (1, 2))
            wait_T("pc")
            emptied("out2", 2)
            for u in range(2):
                post_wait(pe, 12 + u)
                linear_T("cq", u, xT, 2 * u)
            emptied("cq", 2)
            attention(pe, "cross", 8, lambda h, t: [(c_qT[:, 2 * h + m, t * P:(t + 1) * P], c_kT[:, 2 * h + m, :])
                                                    for m in range(2)],
                      lambda h, t, k: c_v[:, k, h * CROSS_D:(h + 1) * CROSS_D], CROSS_D, probs2, probsT2,
                      lambda t: TT)
            transposes("cmix", mix, (1, 2))
            wait_T("cmix")
            for u in range(2):
                post_linear("co", xT, u, 14 + u)
            transposes("pf", xn, (1, 2))
            wait_T("pf")
            emptied("co", 2)
            for u in range(N_GU):
                post_wait(pe, 16 + u)
                w = slot(G2 + 16 + u).rearrange("p (k w c) -> p k w c", k=KD, w=2)
                for m in range(2):
                    j = 2 * u + m
                    if j >= 4:
                        pe.wait_ge(*at("ff_h", j - 3))
                    for gu in range(2):
                        for k in range(KD):
                            i = pe.matmul(bank[j % 4][:, gu * SEQ:(gu + 1) * SEQ], w[:, k, gu, m * P:(m + 1) * P],
                                          xT[:, k, :], start=(k == 0), stop=(k == KD - 1))
                    i.then_inc(S("gu_mm"), 1)
            for half in range(2):
                for n, (k0, k1) in enumerate(FF_PARTS):
                    g = 16 + N_GU + 3 * half + n
                    post_wait(pe, g)
                    if half == 0:
                        pe.wait_ge(*at("ff_h", k1))
                    w = slot(G2 + g)[:, 0:512 * (k1 - k0)].rearrange("p (k c) -> p k c", k=k1 - k0)
                    for t in range(TT):
                        for k in range(k0, k1):
                            i = pe.matmul(bank[4 + 2 * half + t][:, :], ffT[:, k, t * P:(t + 1) * P], w[:, k - k0, :],
                                          start=(k == 0), stop=(k == KF - 1))
                    i.then_inc(S("down_mm"), 1)


        @block.scalar
        def _(act):
            A = nc.scalar.activation
            act_chain = [0]

            def link(i):
                i.then_inc(S("act_chain"), 1)
                act_chain[0] += 1
                act.wait_ge(*at("act_chain", act_chain[0]))

            def squares(name, src, col, junk, ready):
                for t in range(TT):
                    ready(t)
                    A(junk[:, t, :], src[:, t, :], ACT.Square, accum_out=stat[:, col + t:col + t + 1]
                      ).then_inc(S(f"{name}_ss"), 1)

            def evac_T(name, gain=None, dst=xT, scale=1.0, k_total=KD):
                for kp in range(0, k_total // 2, 2):
                    act.wait_ge(*at(f"{name}_tp", kp + 1))
                    for kk in range(2):
                        k = 2 * kp + kk
                        i = A(dst[:, k, :], bank[4][:, kk * SEQ:(kk + 1) * SEQ], ACT.Copy,
                              scale=scale if gain is None else col_gain[:, gain, k:k + 1])
                    i.then_inc(S(f"{name}_Ta"), 1)

            def softmax(name, units, pr, key_tiles):
                heads = units // TT
                for n in range(units):
                    act.wait_ge(*at(f"{name}_nm", n + 1))
                    if n >= 2:
                        act.wait_ge(*at(f"{name}_ptp", n - 1))
                    w = key_tiles(n // heads) * P
                    src = bank[2 + n % 2][:, 0:w] if name != "moba" else pr[:, n % 2, 0:w]
                    A(pr[:, n % 2, 0:w], src, ACT.Exp, bias=negmax[:, n:n + 1],
                      accum_out=esum[:, n:n + 1]).then_inc(S(f"{name}_exp"), 1)

            act.wait_ge(*at("x_in", 16))
            squares("n1", x, 0, mix, lambda t: None)
            act.wait_ge(*at("colgain_in", 80))
            evac_T("n1", 0)

            def in_evac(u):
                c, n = IN_UNITS[u]
                act.wait_ge(*at("in_mm", 2 * u + 1))
                A(proj[:, 0, c:c + n], bank[(2 * u) % 4][:, 0:n], ACT.Copy).then_inc(S("in_ev0"), 1)

            for u in range(3):
                in_evac(u)
            for t in range(TT):
                act.wait_ge(*at("gate_mm", t + 1))
                link(A(gate_tmp[:, 0, t, :], bank[6 + t][:, :], ACT.Abs))
                link(A(gate_tmp[:, 1, t, :], gate_tmp[:, 0, t, :], ACT.Exp, scale=-1.0))
                A(gate_tmp[:, 0, t, :], gate_tmp[:, 1, t, :], ACT.Ln, bias=1.0).then_inc(S("gate_ln"), 1)
            in_evac(3)
            act.wait_ge(*at("gqk_tp", 1))
            A(gqT[:, :, :].rearrange("p r s -> p (r s)"), bank[4][:, :], ACT.Copy, scale=GLA_DK ** -0.5
              ).then_inc(S("gqkT"), 1)
            in_evac(4)
            for i4 in range(4):
                act.wait_ge(*at("sum_mm", i4 + 1))
                b = bank[4 + i4 % 2][:, :]
                A(decay_exp[:, i4, :, :, :].rearrange("p t w c -> p (t w c)"), b, ACT.Exp, scale=1.0 / GATE_NORM)
                A(key_exp[:, i4, :, :], b.rearrange("p (t w c) -> p t w c", t=TT, w=2)[:, :, 0, :], ACT.Exp,
                  scale=-1.0 / GATE_NORM).then_inc(S("sum_exp"), 1)
            for di in range(2):
                act.wait_ge(*at("rest_mm", di + 1))
                A(key_rest[:, di, :, :].rearrange("p t c -> p (t c)"), bank[6 + di][:, :], ACT.Exp,
                  scale=1.0 / GATE_NORM).then_inc(S("rest_exp"), 1)
            act.wait_ge(*at("in_ev0", 4))
            act.wait_ge(*at("in_ev1", 4))
            for t in range(TT):
                A(gqa_tmp[:, t, :, :].rearrange("p h d -> p (h d)"), proj[:, t, C_AQ:C_AV], ACT.Square
                  ).then_inc(S("gqa_sq"), 1)
            act.wait_ge(*at("in_ev0", 5))
            act.wait_ge(*at("in_ev1", 5))
            A(gate_tmp[:, 0, :, :], proj[:, :, C_GG:C_GG + 512], ACT.Exp, scale=-1.0).then_inc(S("gg_exp"), 1)
            for t in range(TT):
                act.wait_ge(*at("gla_o", t + 1))
                for odd in range(2):
                    src = bank[2 * odd + t][:, 0:2 * P].rearrange("p (r d) -> p r d", r=2)
                    for dst, f, name in ((o_gla[:, t, :], ACT.Copy, "gla_oc"), (gate_tmp[:, 1, t, :], ACT.Square, "gla_sq")):
                        A(dst.rearrange("p (r o d) -> p r o d", r=2, o=2)[:, :, odd, :], src, f).then_inc(S(name), 1)
            act.wait_ge(*at("gqa_tp", 1))
            for r in range(2):
                A(gqa_qT[:, 2 * r:2 * r + 2, :].rearrange("p r s -> p (r s)"), bank[4 + r][:, :], ACT.Copy,
                  scale=HD ** -0.5).then_inc(S("gqa_T"), 1)
            softmax("gqa", 16, probs, lambda t: TT)
            squares("att", o_att, 2, xn[:, :, 0:512], lambda t: act.wait_ge(*at("att_o", t + 1)))
            evac_T("mix")
            squares("mm", mem, 36, c_v, lambda t: act.wait_ge(*at("mem_in", 16)))
            evac_T("mm", 2, memT)
            squares("n2", x, 4, mix, lambda t: act.wait_ge(*at(f"out_ev{t}", 2)))
            evac_T("n2")
            act.wait_ge(*at("route_d", 1))
            A(rg[1], rg[0], ACT.Exp).then_inc(S("route_e"), 1)
            act.wait_ge(*at("route_d", 2))
            A(rs[6], rs[5], ACT.Exp).then_inc(S("route_e"), 1)

            act.wait_ge(*at("rounds_ready", 1))
            rounds = act.value_load(rounds_i[0:1, 0:1], min_val=1, max_val=MAX_ROUNDS)
            with act.Fori(0, rounds) as c, act.Fori(0, NB) as b:
                it = c * NB + b
                act.wait_ge(*at("moe_selT_tp", it + 1))
                A(sel_gateT, bank[5][:, 0:SEQ], ACT.Copy).then_inc(S("moe_selT"), 1)
                act.wait_ge(*at("moe_xg_mm", it * 2 + 1))
                A(xg[:, 0:4, :].rearrange("p k s -> p (k s)"), bank[2][:, :], ACT.Copy).then_inc(S("moe_xg_a"), 1)
                for q in range(BATCH):
                    act.wait_ge(*at("moe_gu", it * BATCH + q + 1))
                    A(eg[:, q % 2, :], bank[q % 2][:, 0:P], ACT.Exp, scale=-1.0).then_inc(S("moe_e"), 1)
                    act.wait_ge(*at("moe_hT_tp", it * BATCH + q + 1))
                    A(hT[:, q % 2, :], bank[4][:, 0:P], ACT.Copy).then_inc(S("moe_hT"), 1)
                act.wait_ge(*at("moe_d", it * BATCH + BATCH))
                A(y_batch[:, 0:512], bank[6][:, :], ACT.Copy).then_inc(S("moe_y_a"), 1)
            squares("fin", x, 6, mix, lambda t: act.wait_ge(*at("moe_x", 1)))
            def evac_even(name, n, dst_of, bank_of, scale=1.0):
                for u in range(n):
                    act.wait_ge(*at(f"{name}_mm", 2 * u + 1))
                    A(dst_of(u), bank_of(u), ACT.Copy, scale=scale).then_inc(S(f"{name}_ev0"), 1)

            def two_chunks(dst, j):
                return dst[:, 2 * j:2 * j + 2, :].rearrange("p k s -> p (k s)")

            evac_even("ck", 2, lambda u: two_chunks(c_kT, 2 * u), lambda u: bank[2 * u][:, :])
            squares("pm", x, 38, mix, lambda t: act.wait_ge(*at("x_final", t + 1)))
            evac_even("cv", 2, lambda u: c_v[:, 0, 512 * u:512 * (u + 1)], lambda u: bank[(2 * u) % 4][:, :])
            evac_T("pm", 1)
            evac_even("in2", 6, lambda u: proj2[:, 0, 512 * u:512 * (u + 1)], lambda u: bank[(2 * u) % 4][:, :])
            for r in range(2):
                act.wait_ge(*at("m_tp", r + 1))
                A(two_chunks(m_qT, r), bank[4 + r][:, :], ACT.Copy, scale=HD ** -0.5).then_inc(S("m_T"), 1)
            act.wait_ge(*at("r_tp", 1))
            A(two_chunks(r_qT, 0), bank[0][:, :], ACT.Copy).then_inc(S("r_T"), 1)
            act.wait_ge(*at("rope", 2))
            act.wait_ge(*at("in2_ev1", 6))
            A(ret_g, proj2[:, :, C_RG:C_RG + 512], ACT.Exp, scale=-1.0).then_inc(S("rg_exp"), 1)
            for t in range(TT):
                act.wait_ge(*at("ret_o", t + 1))
                A(ret_o[:, t, :], bank[t][:, :], ACT.Copy).then_inc(S("ret_oc"), 1)
            act.wait_ge(*at("ret_o", TT))
            for t in range(TT):
                A(r_square[:, t, :], bank[t][:, :], ACT.Square).then_inc(S("ret_sq"), 1)
            softmax("moba", 16, probs2, lambda t: t + 1)
            evac_T("mix2")

            def y_half(name, t, done):
                for u in range(2):
                    act.wait_ge(*at(f"{name}_mm", done(u)))
                    A(y[:, t, 512 * u:512 * (u + 1)], bank_y(name, u, t)[:, :], ACT.Copy).then_inc(S(f"{name}_ev{t}"), 1)

            def bank_y(name, u, t):
                return bank[4 + 2 * u + t] if name == "down" else bank[(2 * u + t) % 4]

            def y_squares(name, of, col):
                for t in range(TT):
                    act.wait_ge(*at(f"{name}_ev{t}", 2))
                    A(xn[:, t, :], y[:, t, :], ACT.Square, accum_out=stat[:, col + t:col + t + 1]
                      ).then_inc(S(f"{of}_ss"), 1)

            y_half("out2", 0, lambda u: 2 * u + 1)
            y_squares("out2", "om", 48)
            squares("pc", x, 50, mix, lambda t: act.wait_ge(*at("om_x", t + 1)))
            evac_T("pc", 3)
            evac_even("cq", 2, lambda u: two_chunks(c_qT, 2 * u), lambda u: bank[2 * u][:, :], CROSS_D ** -0.5)
            softmax("cross", 8, probs2, lambda t: TT)
            evac_T("cmix")
            y_half("co", 0, lambda u: 2 * u + 1)
            y_squares("co", "oc", 52)
            squares("pf", x, 54, mix, lambda t: act.wait_ge(*at("oc_x", t + 1)))
            evac_T("pf", 4)
            for j in range(KF):
                act.wait_ge(*at("gu_mm", j + 1))
                if j >= 4:
                    act.wait_ge(*at("ff_h", j - 3))
                A(ff_e[:, j % 4, :], bank[j % 4][:, 0:SEQ], ACT.Exp, scale=-1.0).then_inc(S("ff_exp"), 1)
            y_half("down", 0, lambda u: 3 * (u + 1))
            y_squares("down", "of", 56)

        @block.vector
        def _(dve):
            V = nc.vector
            dve_chain = [0]

            def link(i):
                i.then_inc(S("dve_chain"), 1)
                dve_chain[0] += 1
                dve.wait_ge(*at("dve_chain", dve_chain[0]))

            def scaled(name, src, col, gain=None, dst=xn, signal=None):
                dve.wait_ge(*at(f"{name}_rstd", 1))
                for t in range(TT):
                    r = stat[:, col + t:col + t + 1]
                    if gain is None:
                        i = V.tensor_scalar(dst[:, t, :], src[:, t, :], r, None, ALU.mult)
                    else:
                        i = V.scalar_tensor_tensor(dst[:, t, :], src[:, t, :], r, gain, ALU.mult, ALU.mult)
                    i.then_inc(S(signal or f"{name}_n"), 1)

            def evac_T(name, gain=None, dst=xT, k_total=KD):
                for kp in range(1, k_total // 2, 2):
                    dve.wait_ge(*at(f"{name}_tp", kp + 1))
                    for kk in range(2):
                        k = 2 * kp + kk
                        src = bank[5][:, kk * SEQ:(kk + 1) * SEQ]
                        if gain is None:
                            i = V.tensor_copy(dst[:, k, :], src)
                        else:
                            i = V.tensor_scalar(dst[:, k, :], src, col_gain[:, gain, k:k + 1], None, ALU.mult)
                    i.then_inc(S(f"{name}_Tv"), 1)

            def attend(name, units, prT, key_tiles, maximum):
                heads = units // TT
                for n in range(units + 1):
                    if n < units:
                        dve.wait_ge(*at(f"{name}_sc", n + 1))
                        maximum(n)
                    if n >= 1:
                        m = n - 1
                        dve.wait_ge(*at(f"{name}_ptp", m + 1))
                        if m >= 2:
                            dve.wait_ge(*at(f"{name}_pv", m - 1))
                        w = key_tiles(m // heads) * P
                        V.tensor_copy(prT[:, m % 2, 0:w], bank[6 + m % 2][:, 0:w]).then_inc(S(f"{name}_PT"), 1)

            def plain_max(name):
                return lambda n: V.tensor_reduce(negmax[:, n:n + 1], bank[2 + n % 2][:, 0:SEQ], AX.X, ALU.max,
                                                 negate=True).then_inc(S(f"{name}_nm"), 1)

            scaled("n1", x, 0)
            dve.wait_ge(*at("colgain_in", 80))
            evac_T("n1", 0)

            def in_evac(u):
                c, n = IN_UNITS[u]
                dve.wait_ge(*at("in_mm", 2 * u + 2))
                V.tensor_copy(proj[:, 1, c:c + n], bank[(2 * u + 1) % 4][:, 0:n]).then_inc(S("in_ev1"), 1)

            in_evac(0)
            in_evac(1)
            dve.wait_ge(*at("zT_one", 1))
            dve.wait_ge(*at("zT_tp", 1))
            V.tensor_copy(zT[0:32, :], bank[4][0:32, 0:SEQ]).then_inc(S("zT_ev"), 1)
            in_evac(2)
            for t in range(TT):
                dve.wait_ge(*at("gate_ln", t + 1))
                V.scalar_tensor_tensor(la[:, t, :], bank[6 + t][:, :], 0.0, gate_tmp[:, 0, t, :], ALU.min,
                                       ALU.subtract).then_inc(S("la"), 1)
            in_evac(3)
            dve.wait_ge(*at("gqk_tp", 2))
            V.tensor_copy(gkT[:, :, :].rearrange("p r s -> p (r s)"), bank[5][:, :]).then_inc(S("gqkT"), 1)
            in_evac(4)
            dve.wait_ge(*at("gqkT", 2))
            for i4 in range(4):
                di, r = i4 // 2, i4 % 2
                dve.wait_ge(*at("sum_exp", i4 + 1))
                last = slice(63, 128, 64) if di == 0 else slice(0, 128, 64)
                link(V.tensor_copy(chunk_decay[:, i4, :].rearrange("p (t c) -> p t c", t=TT),
                                   decay_exp[:, i4, :, 1, last]))
                q = gqT[:, r, :].rearrange("p (t c) -> p t c", t=TT)
                k = gkT[:, r, :].rearrange("p (t c) -> p t c", t=TT)
                V.tensor_tensor(decay_exp[:, i4, :, 0, :], decay_exp[:, i4, :, 0, :], q, ALU.mult)
                V.tensor_tensor(decay_exp[:, i4, :, 1, :], decay_exp[:, i4, :, 1, :], q, ALU.mult)
                V.tensor_tensor(key_exp[:, i4, :, :], key_exp[:, i4, :, :], k, ALU.mult).then_inc(S("gla_qk"), 1)
            dve.wait_ge(*at("in_ev0", 5))
            for di in range(2):
                dve.wait_ge(*at("rest_exp", di + 1))
                V.tensor_tensor(key_rest[:, di, :, :], key_rest[:, di, :, :], proj[:, :, C_GK:C_GK + 256], ALU.mult
                                ).then_inc(S("key_rest"), 1)
            dve.wait_ge(*at("mask_in", 16))
            dve.wait_ge(*at("scores_zero", 1))
            for h in range(GLA_H):
                dve.wait_ge(*at("gla_sc", h + 1))
                V.copy_predicated(scores[:, h, :], gla_mask[:, :], bank[h][:, :]).then_inc(S("gla_masked"), 1)
            for n in range(3):
                for i4 in range(4):
                    ch = n if i4 < 2 else 3 - n
                    if n == 0:
                        dve.wait_ge(*at("gla_kv", 4))
                        i = V.tensor_copy(state[:, i4, 0, :], kv_of(i4, ch))
                    else:
                        i = V.scalar_tensor_tensor(state[:, i4, n, :], state[:, i4, n - 1, :],
                                                   chunk_decay[:, i4, ch:ch + 1], kv_of(i4, ch),
                                                   ALU.mult, ALU.add)
                    if n < 2 and i4 == 3:
                        link(i)
                    elif n == 2:
                        i.then_inc(S("gla_state"), 1)
            NH = GQA_H + GQA_KV
            qk = proj[:, :, C_AQ:C_AV].rearrange("p t (h d) -> p t h d", d=HD)
            dve.wait_ge(*at("gqa_sq", TT))
            V.tensor_reduce(stat[:, 16:16 + TT * NH].rearrange("p (t h) -> p t h", t=TT), gqa_tmp, AX.X, ALU.add
                            ).then_inc(S("gqa_ss"), 1)
            dve.wait_ge(*at("gqa_rstd", 1))
            r = stat[:, 16:16 + TT * NH].rearrange("p (t h) -> p t h", t=TT).unsqueeze(3).to_broadcast([P, TT, NH, HD])
            link(V.tensor_tensor(qk, qk, r, ALU.mult))
            dve.wait_ge(*at("qkgain_in", 32))
            for a, b, g in ((0, GQA_H, 0), (GQA_H, NH, HD)):
                gain = qk_gain[:, g:g + HD].unsqueeze(1).unsqueeze(1).to_broadcast([P, TT, b - a, HD])
                i = V.tensor_tensor(qk[:, :, a:b, :], qk[:, :, a:b, :], gain, ALU.mult)
            link(i)

            def table(name, n):
                return C1(name).rearrange("p (t d) -> p t d", t=TT).unsqueeze(2).to_broadcast([P, TT, NH, n])

            V.tensor_tensor(gqa_tmp[:, :, :, 0:HD:2], qk[:, :, :, 1:HD:2], table("gqa_nsin", HD // 2), ALU.mult)
            link(V.tensor_tensor(gqa_tmp[:, :, :, 1:HD:2], qk[:, :, :, 0:HD:2], table("gqa_sin", HD // 2), ALU.mult))
            link(V.tensor_tensor(qk, qk, table("gqa_cos", HD), ALU.mult))
            link(V.tensor_tensor(qk, qk, gqa_tmp, ALU.add))
            for u in range(2):
                i = V.tensor_copy(kdup[:, :, :, u, :], qk[:, :, GQA_H:NH, :])
            i.then_inc(S("gqa_qk"), 1)
            dve.wait_ge(*at("gg_exp", 1))
            sg = gate_tmp[:, 0, :, :]
            link(V.tensor_scalar(sg, sg, 1.0, None, ALU.add))
            link(V.reciprocal(sg, sg))
            link(V.tensor_tensor(sg, sg, proj[:, :, C_GG:C_GG + 512], ALU.mult))
            dve.wait_ge(*at("glagain_in", 16))
            sgh = sg.rearrange("p t (h d) -> p (t h) d", h=GLA_H)
            link(V.tensor_tensor(sgh, sgh, gla_gain.unsqueeze(1).to_broadcast([P, TT * GLA_H, GLA_DV]), ALU.mult))
            dve.wait_ge(*at("gla_sq", 2 * TT))
            V.tensor_reduce(stat[:, 8:16], gate_tmp[:, 1, :, :].rearrange("p t (h d) -> p (t h) d", h=GLA_H), AX.X,
                            ALU.add).then_inc(S("gla_ss"), 1)
            dve.wait_ge(*at("gqa_tp", 1))
            V.tensor_copy(gqa_kT[:, :, :].rearrange("p r s -> p (r s)"), bank[6][:, :]).then_inc(S("gqa_T"), 1)
            dve.wait_ge(*at("gla_rstd", 1))
            og = o_gla[:, :, :].rearrange("p t (h d) -> p (t h) d", h=GLA_H)
            link(V.tensor_tensor(og, og, stat[:, 8:16].unsqueeze(2).to_broadcast([P, TT * GLA_H, GLA_DV]), ALU.mult))
            link(V.tensor_tensor(mix[:, 0, 0:512], o_gla[:, 0, :], sg[:, 0, :], ALU.mult))
            link(V.tensor_tensor(mix[:, 1, 0:512], o_gla[:, 1, :], sg[:, 1, :], ALU.mult))
            attend("gqa", 16, probsT, lambda t: TT, plain_max("gqa"))
            for t in range(TT):
                dve.wait_ge(*at("gqa_pv", 8 * (t + 1)))
                link(V.reciprocal(ersum[:, 8 * t:8 * t + 8], esum[:, 8 * t:8 * t + 8]))
                V.tensor_tensor(o_att[:, t, :].rearrange("p (h d) -> p h d", d=HD),
                                bank[4 + t][:, :].rearrange("p (h d) -> p h d", d=HD),
                                ersum[:, 8 * t:8 * t + 8].unsqueeze(2).to_broadcast([P, 8, HD]), ALU.mult
                                ).then_inc(S("att_o"), 1)
            dve.wait_ge(*at("attgain_in", 16))
            scaled("att", o_att, 2, att_gain, mix[:, :, 512:1024], "mix_n")
            evac_T("mix")

            def add_out(name, t, u):
                xs = x[:, t, 512 * u:512 * (u + 1)]
                dve.wait_ge(*at(f"{name}_mm", 2 * u + t + 1))
                V.tensor_tensor(xs, xs, bank[(2 * u + t) % 4][:, :], ALU.add).then_inc(S(f"{name}_ev{t}"), 1)

            for u in range(2):
                for t in range(TT):
                    add_out("out", t, u)
                if u == 0:
                    scaled("mm", mem, 36, dst=mem)
                    evac_T("mm", 2, memT)
            dve.wait_ge(*at("norm2gain_in", 16))
            scaled("n2", x, 4, row_gain[:, 0, :])
            evac_T("n2")

            dve.wait_ge(*at("route_mm", 1))
            for t in range(TT):
                i = V.tensor_copy(logits[:, t, :], bank[t][:, 0:72])
            link(i)
            lg, le = logits[:, :, 0:NG], logits[:, :, NG:]
            rank8 = C1("rank8").unsqueeze(1).to_broadcast([P, TT, NG])
            rank64 = C1("rank64").unsqueeze(1).to_broadcast([P, TT, NE])

            def over(v, n):
                return v.unsqueeze(2).to_broadcast([P, TT, n])

            def first_max(dst, src, n, rank, top, tmp):
                link(V.tensor_reduce(top, src, AX.X, ALU.max))
                link(V.tensor_tensor(tmp, src, over(top, n), ALU.is_equal))
                link(V.tensor_tensor(tmp, tmp, rank, ALU.mult))
                link(V.tensor_reduce(rs[11], tmp, AX.X, ALU.max))
                link(V.tensor_tensor(dst, tmp, over(rs[11], n), ALU.is_equal))

            first_max(rg[2], lg, NG, rank8, rs[0], rg[3])
            V.tensor_tensor(rg[0], lg, over(rs[0], NG), ALU.subtract).then_inc(S("route_d"), 1)
            link(V.tensor_scalar(rg[3], rg[2], -NEG, NEG, ALU.mult, ALU.add))
            link(V.tensor_tensor(rt[0].rearrange("p t (g e) -> p t g e", g=NG), le.rearrange("p t (g e) -> p t g e", g=NG),
                                 rg[3].unsqueeze(3).to_broadcast([P, TT, NG, EPG]), ALU.add))
            first_max(rt[1], rt[0], NE, rank64, rs[1], rt[2])
            link(V.scalar_tensor_tensor(rt[3].rearrange("p t e -> p (t e)"), rt[1].rearrange("p t e -> p (t e)"), -3e38,
                                        rt[0].rearrange("p t e -> p (t e)"), ALU.mult, ALU.add))
            first_max(rt[4], rt[3], NE, rank64, rs[2], rt[2])
            V.tensor_tensor(picked, rt[1], rt[4], ALU.add).then_inc(S("picked"), 1)
            V.tensor_tensor(rs[5], rs[2], rs[1], ALU.subtract).then_inc(S("route_d"), 1)
            dve.wait_ge(*at("route_e", 1))
            link(V.tensor_reduce(rs[3], rg[1], AX.X, ALU.add))
            link(V.reciprocal(rs[4], rs[3]))
            dve.wait_ge(*at("route_e", 2))
            link(V.tensor_scalar(rs[7], rs[6], 1.0, None, ALU.add))
            link(V.reciprocal(rs[8], rs[7]))
            link(V.tensor_tensor(rs[9], rs[4], rs[8], ALU.mult))
            link(V.tensor_tensor(rs[10], rs[9], rs[6], ALU.mult))
            link(V.tensor_tensor(rt[1], rt[1], over(rs[9], NE), ALU.mult))
            link(V.tensor_tensor(rt[4], rt[4], over(rs[10], NE), ALU.mult))
            link(V.tensor_tensor(gate_of, rt[1], rt[4], ALU.add))
            dve.wait_ge(*at("place_mm", 1))
            link(V.tensor_tensor(rt[0], bank[2][:, 0:2 * NE].rearrange("p (t e) -> p t e", t=TT), picked, ALU.mult))
            link(V.tensor_scalar(rt[2], picked, -1.0, None, ALU.add))
            link(V.tensor_tensor(place, rt[0], rt[2], ALU.add))
            link(V.tensor_reduce(rs[3][0:1, 0:1], bank[2][0:1, 2 * NE:3 * NE], AX.X, ALU.max))
            link(V.tensor_scalar(rounds_f[0:1, 0:7], C1("rounds")[0:1, :], rs[3][0:1, 0:1], 1.0, ALU.is_lt, ALU.add,
                                 accum_out=rounds_f[0:1, 7:8]))
            V.tensor_copy(rounds_i[0:1, 0:1], rounds_f[0:1, 7:8]).then_inc(S("rounds_ready"), 1)
            link(V.tensor_copy(slots_now, C1("slot")))

            V.memset(stat[:, 120:121], 0.0).then_inc(S("moe_xadd"), 1)
            dve.wait_ge(*at("rounds_ready", 1))
            rounds = dve.value_load(rounds_i[0:1, 0:1], min_val=1, max_val=MAX_ROUNDS)
            LINKS = 3 * BATCH + 2
            with dve.Fori(0, rounds) as c:
                with dve.Fori(0, NB) as b:
                    it = c * NB + b
                    links = [0]

                    def mlink(i):
                        i.then_inc(S("moe_chain"), 1)
                        links[0] += 1
                        dve.wait_ge(*at("moe_chain", it * LINKS + links[0]))

                    for t in range(TT):
                        mlink(V.tensor_tensor(
                            sel[:, t, :].rearrange("p (q j) -> p q j", q=BATCH),
                            slots_now.unsqueeze(1).to_broadcast([P, BATCH, TOK]),
                            place[:, t, bass.ds(b * BATCH, BATCH)].unsqueeze(2).to_broadcast([P, BATCH, TOK]),
                            ALU.is_equal))
                        i = V.tensor_tensor(
                            sel_gate[:, t, :].rearrange("p (q j) -> p q j", q=BATCH),
                            sel[:, t, :].rearrange("p (q j) -> p q j", q=BATCH),
                            gate_of[:, t, bass.ds(b * BATCH, BATCH)].unsqueeze(2).to_broadcast([P, BATCH, TOK]),
                            ALU.mult)
                    i.then_inc(S("moe_sel"), 1)
                    dve.wait_ge(*at("moe_xg_mm", it * 2 + 2))
                    V.tensor_copy(xg[:, 4:8, :].rearrange("p k s -> p (k s)"), bank[3][:, :]).then_inc(S("moe_xg_v"), 1)
                    for q in range(BATCH):
                        dve.wait_ge(*at("moe_e", it * BATCH + q + 1))
                        mlink(V.tensor_scalar(eg[:, q % 2, :], eg[:, q % 2, :], 1.0, None, ALU.add))
                        mlink(V.reciprocal(hr, eg[:, q % 2, :]))
                        mlink(V.tensor_tensor(hr, hr, bank[q % 2][:, 0:P], ALU.mult))
                        V.tensor_tensor(hx[:, q % 2, :], hr, bank[q % 2][:, P:2 * P], ALU.mult).then_inc(S("moe_h"), 1)
                    dve.wait_ge(*at("moe_d", it * BATCH + BATCH))
                    V.tensor_copy(y_batch[:, 512:1024], bank[7][:, :]).then_inc(S("moe_y_v"), 1)
                    for n in range(4):
                        half, t = n // 2, n % 2
                        xs = x[:, t, half * 512:(half + 1) * 512]
                        dve.wait_ge(*at("moe_cmb", it * 4 + n + 1))
                        V.tensor_tensor(xs, xs, bank[2 + n % 2][:, :], ALU.add).then_inc(S("moe_xadd"), 1)
                    assert links[0] == LINKS
                V.tensor_scalar(slots_now, slots_now, float(TOK), None, ALU.add).then_inc(S("moe_round"), 1)
                dve.wait_ge(*at("moe_round", c + 1))
            dve.wait_ge(*at("moe_xadd", rounds * (4 * NB) + 1))
            V.memset(stat[:, 121:122], 0.0).then_inc(S("moe_x"), 1)
            dve.wait_ge(*at("finalgain_in", 16))
            scaled("fin", x, 6, row_gain[:, 1, :], x, "x_final")
            def evac_odd(name, n, dst_of, bank_of, scale=None):
                for u in range(n):
                    dve.wait_ge(*at(f"{name}_mm", 2 * u + 2))
                    if scale is None:
                        i = V.tensor_copy(dst_of(u), bank_of(u))
                    else:
                        i = V.tensor_scalar(dst_of(u), bank_of(u), scale, None, ALU.mult)
                    i.then_inc(S(f"{name}_ev1"), 1)

            def two_chunks(dst, j):
                return dst[:, 2 * j:2 * j + 2, :].rearrange("p k s -> p (k s)")

            evac_odd("ck", 2, lambda u: two_chunks(c_kT, 2 * u + 1), lambda u: bank[2 * u + 1][:, :])
            scaled("pm", x, 38)
            evac_odd("cv", 2, lambda u: c_v[:, 1, 512 * u:512 * (u + 1)], lambda u: bank[(2 * u + 1) % 4][:, :])
            evac_T("pm", 1)
            evac_odd("in2", 6, lambda u: proj2[:, 1, 512 * u:512 * (u + 1)], lambda u: bank[(2 * u + 1) % 4][:, :])
            dve.wait_ge(*at("in2_ev0", 6))
            dve.wait_ge(*at("c2_in", 16))
            for c0, nh, hw, name in ((C_MQ, 2 * MOBA_H, 8, "moba"), (C_RQ, 2 * RET_H, 32, "ret")):
                v = proj2[:, :, c0:c0 + nh * HD].rearrange("p t (h d) -> p t h d", d=HD)
                lo, hi = v[:, :, :, 0:hw], v[:, :, :, hw:2 * hw]
                cos, sin = (C2(f"{name}_{f}").rearrange("p (t d) -> p t d", t=TT).unsqueeze(2)
                            .to_broadcast([P, TT, nh, hw]) for f in ("cos", "sin"))
                tmp = [rope_tmp[:, n, :, 0:nh * hw].rearrange("p t (h d) -> p t h d", d=hw) for n in range(4)]
                if name == "ret":
                    dve.wait_ge(*at("rope", 1))
                for n, (a, b) in enumerate(((lo, cos), (hi, sin), (hi, cos), (lo, sin))):
                    i = V.tensor_tensor(tmp[n], a, b, ALU.mult)
                link(i)
                link(V.tensor_tensor(lo, tmp[0], tmp[1], ALU.subtract))
                V.tensor_tensor(hi, tmp[2], tmp[3], ALU.add).then_inc(S("rope"), 1)
            for r in range(2):
                dve.wait_ge(*at("m_tp", 3 + r))
                V.tensor_copy(two_chunks(m_kT, r), bank[6 + r][:, :]).then_inc(S("m_T"), 1)
            dve.wait_ge(*at("r_tp", 2))
            V.tensor_copy(two_chunks(r_kT, 0), bank[1][:, :]).then_inc(S("r_T"), 1)
            W = SEQ + P
            for h in range(RET_H):
                dve.wait_ge(*at("ret_sc", h + 1))
                V.tensor_tensor(r_scores[:, h, :], bank[h][:, 0:W], C2("decay", h * W, (h + 1) * W), ALU.mult
                                ).then_inc(S("ret_decayed"), 1)
            dve.wait_ge(*at("rg_exp", 1))
            link(V.tensor_scalar(ret_g, ret_g, 1.0, None, ALU.add))
            link(V.reciprocal(ret_g, ret_g))
            link(V.tensor_tensor(ret_g, ret_g, proj2[:, :, C_RG:C_RG + 512], ALU.mult))
            dve.wait_ge(*at("ret_sq", TT))
            V.tensor_reduce(stat[:, 40:48], r_square[:, :, :].rearrange("p t (h d) -> p (t h) d", h=RET_H), AX.X,
                            ALU.add).then_inc(S("ret_ss"), 1)
            dve.wait_ge(*at("ret_rstd", 1))
            ro = ret_o[:, :, :].rearrange("p t (h d) -> p (t h) d", h=RET_H)
            link(V.tensor_tensor(ro, ro, stat[:, 40:48].unsqueeze(2).to_broadcast([P, TT * RET_H, RET_DV]), ALU.mult))
            link(V.tensor_tensor(mix[:, :, 512:1024], ret_o, ret_g, ALU.mult))

            def masked_max(n):
                w = (n // MOBA_H + 1) * P
                link(V.tensor_tensor_reduce(probs2[:, n % 2, 0:w], bank[2 + n % 2][:, 0:w], C2("causal", 2 * P - w, 2 * P),
                                            1.0, -3e38, ALU.add, ALU.max, ersum[:, n:n + 1]))
                V.tensor_scalar(negmax[:, n:n + 1], ersum[:, n:n + 1], -1.0, None, ALU.mult).then_inc(S("moba_nm"), 1)

            attend("moba", 16, probsT2, lambda t: t + 1, masked_max)
            for t in range(TT):
                dve.wait_ge(*at("moba_pv", MOBA_H * (t + 1)))
                link(V.reciprocal(ersum[:, 8 * t:8 * t + 8], esum[:, 8 * t:8 * t + 8]))
                V.tensor_tensor(mix[:, t, 0:512].rearrange("p (h d) -> p h d", d=HD),
                                bank[4 + t][:, :].rearrange("p (h d) -> p h d", d=HD),
                                ersum[:, 8 * t:8 * t + 8].unsqueeze(2).to_broadcast([P, 8, HD]), ALU.mult
                                ).then_inc(S("mix2_n"), 1)
            evac_T("mix2")

            def y_half(name, done, bank_of):
                for u in range(2):
                    dve.wait_ge(*at(f"{name}_mm", done(u)))
                    V.tensor_copy(y[:, 1, 512 * u:512 * (u + 1)], bank_of(u)[:, :]).then_inc(S(f"{name}_ev1"), 1)

            def add_normed(of, col, row, signal):
                dve.wait_ge(*at(f"{of}_rstd", 1))
                for t in range(TT):
                    link(V.scalar_tensor_tensor(y[:, t, :], y[:, t, :], stat[:, col + t:col + t + 1], row_gain[:, row, :],
                                                ALU.mult, ALU.mult))
                    V.tensor_tensor(x[:, t, :], x[:, t, :], y[:, t, :], ALU.add).then_inc(S(signal), 1)

            y_half("out2", lambda u: 2 * u + 2, lambda u: bank[(2 * u + 1) % 4])
            dve.wait_ge(*at("postmix_in", 16))
            add_normed("om", 48, 0, "om_x")
            scaled("pc", x, 50)
            evac_T("pc", 3)
            evac_odd("cq", 2, lambda u: two_chunks(c_qT, 2 * u + 1), lambda u: bank[2 * u + 1][:, :], CROSS_D ** -0.5)
            attend("cross", 8, probsT2, lambda t: TT, plain_max("cross"))
            for t in range(TT):
                dve.wait_ge(*at("cross_pv", CROSS_H * (t + 1)))
                link(V.reciprocal(ersum[:, 4 * t:4 * t + 4], esum[:, 4 * t:4 * t + 4]))
                for r in range(2):
                    i = V.tensor_tensor(mix[:, t, 512 * r:512 * (r + 1)].rearrange("p (h d) -> p h d", h=2),
                                        bank[(4 if t == 0 else 0) + r][:, :].rearrange("p (h d) -> p h d", h=2),
                                        ersum[:, 4 * t + 2 * r:4 * t + 2 * r + 2].unsqueeze(2)
                                        .to_broadcast([P, 2, CROSS_D]), ALU.mult)
                i.then_inc(S("cmix_n"), 1)
            evac_T("cmix")
            y_half("co", lambda u: 2 * u + 2, lambda u: bank[(2 * u + 1) % 4])
            dve.wait_ge(*at("postcross_in", 16))
            add_normed("oc", 52, 1, "oc_x")
            scaled("pf", x, 54)
            evac_T("pf", 4)
            for j in range(KF):
                e = ff_e[:, j % 4, :]
                dve.wait_ge(*at("ff_exp", j + 1))
                link(V.tensor_scalar(e, e, 1.0, None, ALU.add))
                link(V.reciprocal(e, e))
                link(V.tensor_tensor(e, e, bank[j % 4][:, 0:SEQ], ALU.mult))
                V.tensor_tensor(ffT[:, j, :], e, bank[j % 4][:, SEQ:2 * SEQ], ALU.mult).then_inc(S("ff_h"), 1)
            y_half("down", lambda u: 3 * (u + 1), lambda u: bank[5 + 2 * u])
            dve.wait_ge(*at("postffn_in", 16))
            add_normed("of", 56, 0, "ffn_x")


_INS = ["x", "norm1_gain", "w_in", "gla_up_fwd", "gla_up_fwd_bias", "gla_up_bwd", "gla_up_bwd_bias", "gla_out_gain",
        "q_norm_gain", "k_norm_gain", "att_out_gain", "w_out", "norm2_gain", "w_group", "b_group", "w_expert",
        "b_expert", "w_gate", "w_up", "w_down", "final_gain", "mem_2", "g_pre_mix_2", "w_in_2", "w_out_2",
        "g_post_mix_2", "g_pre_cross_2", "g_mem_2", "w_cq_2", "w_ckv_2", "w_co_2", "g_post_cross_2", "g_pre_ffn_2",
        "w_gate_up_2", "w_down_2", "g_post_ffn_2"]


def kernel(**inputs):
    import concourse.bacc as _bacc
    from concourse.bass_utils import run_bass_kernel_spmd as _run

    nc = _bacc.Bacc("TRN2", target_bir_lowering=False, num_devices=1)
    arrays, t_in = {}, {}

    def dram(name, a):
        arrays[name] = a
        return nc.dram_tensor(name, a.shape, mybir.dt.from_np(a.dtype), kind="ExternalInput").ap()

    for name in _INS:
        t_in[name] = dram(f"in_{name}_dram", np.ascontiguousarray(inputs[name]))
    c1, c1_at, c2, c2_at, mask = shape_constants()
    consts = {"c1": dram("const_1", c1), "c2": dram("const_2", c2), "mask": dram("const_mask", mask),
              "c1_at": c1_at, "c2_at": c2_at}
    out = nc.dram_tensor("out_0_dram", (1, SEQ, D), F32, kind="ExternalOutput").ap()
    build(nc, t_in, consts, out)
    r = _run(nc, [arrays], core_ids=[0])
    return r.results[0]["out_0_dram"]
```

```python
from contextlib import ExitStack

import numpy as np

import concourse.bass as bass
from concourse import mybir

F32 = mybir.dt.float32
I32 = mybir.dt.int32
ALU = mybir.AluOpType
ACT = mybir.ActivationFunctionType
AX = mybir.AxisListType

P = 128
SEQ, D = 256, 1024
TT = SEQ // P
KD = D // P
EPS = 1e-6

GLA_H, GLA_DK, GLA_DV, GLA_CHUNK, GLA_RANK = 4, 64, 128, 64, 16
GATE_NORM = 16.0
GQA_H, GQA_KV, HD = 8, 2, 64
NG, EPG, NE, F_EXP = 8, 8, 64, 512
D_IN = 2336
C_GQ, C_GK, C_GV, C_GG, C_Z, C_AQ, C_AK, C_AV = 0, 256, 512, 1024, 1536, 1568, 2080, 2208

D_IN2 = 3072
C_MQ, C_MK, C_MV, C_RQ, C_RK, C_RV, C_RG = 0, 512, 1024, 1536, 1792, 2048, 2560
IN2_UNITS = [C_MQ, C_MK, C_RQ, C_MV, C_RV, C_RG]
MOBA_H, RET_H, RET_DK, RET_DV = 8, 4, 64, 128
CROSS_H, CROSS_D = 4, 256
D_FF = 2816
KF = D_FF // P
GU_COLS = 256
N_GU = D_FF // GU_COLS

RING, SLOT = 6, 4096
TOK = 32
BATCH = 4
NB = NE // BATCH
MAX_ROUNDS = SEQ // TOK
NEG = -1e30

IN_UNITS = [(C, min(512, D_IN - C)) for C in (1536, 0, 512, 2048, 1024)]
OUT_UNITS = [(0, 512), (512, 512)]
CK_UNITS = [(0, 512), (512, 512)]
PRE_UNITS = len(IN_UNITS) + len(OUT_UNITS) + len(CK_UNITS)
MOE_UNITS = [("a", 0), ("b", 0), ("a", 1), ("b", 1), ("d", 0), ("a", 2), ("b", 2), ("d", 1), ("a", 3), ("b", 3),
             ("d", 2), ("d", 3)]
CK_BANKS = (2, 6, 7, 4)
assert len(MOE_UNITS) == 2 * RING


def shape_constants():
    f = np.float32
    i = np.arange(P)
    s, t = i[:, None], i[None, :]
    same = (s // GLA_CHUNK) == (t // GLA_CHUNK)
    half = GLA_CHUNK // 2
    fwd = same & (s <= t)
    bwd = same & (s >= t)
    ref_f = same & (s % GLA_CHUNK <= half - 1)
    ref_b = same & (s % GLA_CHUNK >= half)
    cols = {
        "ident": np.eye(P, dtype=f),
        "cum_f": np.concatenate([fwd.astype(f) - ref_f, fwd], 1),
        "cum_b": np.concatenate([bwd.astype(f) - ref_b, bwd], 1),
        "rest_f": same & (s > t),
        "rest_b": same & (s < t),
        "before": s < t,
        "ones": np.ones((P, P)),
        "rank8": np.tile(NG - np.arange(NG), (P, 1)),
        "rank64": np.tile(NE - np.arange(NE), (P, 1)),
        "slot": np.tile(np.arange(TOK), (P, 1)),
        "neghalf": np.full((P, 32), -0.5),
        "rounds": np.tile(TOK * np.arange(1, MAX_ROUNDS), (P, 1)),
    }
    pos = np.arange(SEQ)
    inv = (f(10000.0) ** (-np.arange(0, 32, 2, dtype=f) / f(32))).astype(f)
    ang = np.concatenate([(pos // 64).astype(f)[:, None] * inv, (pos % 64).astype(f)[:, None] * inv], -1).astype(f)
    cos, sin = np.cos(ang).astype(f), np.sin(ang).astype(f)
    by_tile = lambda a: a.reshape(TT, P, -1).transpose(1, 0, 2).reshape(P, -1)
    cols["gqa_cos"] = by_tile(np.repeat(cos, 2, axis=1))
    cols["gqa_sin"] = by_tile(sin)
    cols["gqa_nsin"] = by_tile(-sin)
    at, n = {}, 0
    for name, a in cols.items():
        at[name] = (n, n + a.shape[1])
        n += a.shape[1]
    c1 = np.concatenate([np.asarray(a, f) for a in cols.values()], 1)

    causal = np.where(t <= s, 0.0, NEG)
    cols2 = {"causal": np.concatenate([np.zeros((P, P)), causal], 1)}
    inv_m = (f(500000.0) ** (-np.arange(8, dtype=f) * f(2.0) / f(16))).astype(f)
    am = (pos.astype(f)[:, None] * inv_m).astype(f)
    inv_r = (f(1.0) / (f(10000.0) ** np.linspace(0.0, 1.0, RET_DK // 2, dtype=f))).astype(f)
    ar = (pos.astype(f)[:, None] * inv_r).astype(f)
    cols2["moba_cos"], cols2["moba_sin"] = by_tile(np.cos(am).astype(f)), by_tile(np.sin(am).astype(f))
    cols2["ret_cos"], cols2["ret_sin"] = by_tile(np.cos(ar).astype(f)), by_tile(np.sin(ar).astype(f))
    q, k = np.arange(SEQ)[None, :], np.arange(SEQ)[:, None]
    dec = []
    for h in range(RET_H):
        log_g = np.log(1.0 - 2.0 ** (-5.0 - h))
        m = np.where(q >= k, np.exp(log_g * np.maximum(q - k, 0)), 0.0) * RET_DK ** -0.5
        dec += [m[:P, :], m[P:, P:]]
    cols2["decay"] = np.concatenate(dec, 1)
    at2, n = {}, 0
    for name, a in cols2.items():
        at2[name] = (n, n + a.shape[1])
        n += a.shape[1]
    c2 = np.concatenate([np.asarray(a, f) for a in cols2.values()], 1)

    mask = np.concatenate([fwd, fwd, bwd, bwd], 1).astype(np.int32)
    return c1, at, c2, at2, mask


def build(nc, t_in, consts, out):
    c1_at, c2_at = consts["c1_at"], consts["c2_at"]
    with ExitStack() as ctx:
        def sb(name, cols, dt=F32):
            return ctx.enter_context(nc.sbuf_tensor(name, [P, cols], dt))

        sems, counted = {}, {}
        for signal, stages in (
                ("ss", "n1 att mm n2 fin pm om+pc oc+pf of"),
                ("rstd", "n1 gqa gla att mm n2 fin pm ret om+pc oc+pf of"),
                ("n", "n1 mix mm n2 pm mix2 pc cmix pf"),
                ("tp", "n1 mix mm n2 pm mix2 pc cmix pf"),
                ("Ta", "n1 mix mm n2 pm mix2 pc cmix pf"),
                ("Tv", "n1 mix mm n2 pm mix2 pc cmix pf")):
            base = 0
            for group in stages.split():
                names = group.split("+")
                for i, stage in enumerate(names):
                    counted[f"{stage}_{signal}"] = ("all_" + signal, base + i + 1 - len(names), len(names))
                base += (1 if group in ("gqa", "gla", "ret") else TT) * len(names)
        for signal, counts in (("mm", (10, 4, 4, 4, 12, 4, 4, 4)), ("ev0", (5, 2, 2, 2, 6, 2, 2, 2)),
                               ("ev1", (5, 2, 2, 2, 6, 2, 2, 2))):
            base = 0
            for stage, n in zip("in out ck cv in2 out2 cq co".split(), counts):
                if (stage, signal) != ("out", "ev0"):
                    counted[f"{stage}_{signal}"] = ("all_" + signal, base, 1)
                    base += n

        def S(name):
            name = counted.get(name, (name,))[0]
            if name not in sems:
                sems[name] = ctx.enter_context(nc.semaphore(name))
            return sems[name]

        def at(name, value):
            _, base, stride = counted.get(name, (name, 0, 1))
            return S(name), base + stride * value

        ring = sb("ring", RING * SLOT)
        x = sb("x", TT * D).rearrange("p (t d) -> p t d", t=TT)
        xn = sb("xn", TT * D).rearrange("p (t d) -> p t d", t=TT)
        xT_ = sb("xT", KD * SEQ)
        xT = xT_.rearrange("p (k s) -> p k s", k=KD)
        mix_ = sb("mix", TT * D)
        mix = mix_.rearrange("p (t d) -> p t d", t=TT)
        big = sb("big", 6144)
        aux = sb("aux", 7680)
        c1 = sb("c1", consts["c1"].shape[1])
        c2 = sb("c2", consts["c2"].shape[1])
        gla_mask = sb("gla_mask", 4 * P, I32)
        row_gain = sb("row_gain", 2 * D).rearrange("p (r d) -> p r d", r=2)
        col_gain = sb("col_gain", 5 * KD).rearrange("p (r k) -> p r k", r=5)
        stat = sb("stat", 128)
        rounds_i = sb("rounds_i", 1, I32)

        def C1(name, lo=0, hi=None):
            a, b = c1_at[name]
            return c1[:, a + lo:(b if hi is None else a + hi)]

        def C2(name, lo=0, hi=None):
            a, b = c2_at[name]
            return c2[:, a + lo:(b if hi is None else a + hi)]

        ident = C1("ident")

        bank = [ctx.enter_context(nc.psum_tensor(f"bank{i}", [P, 512], F32)) for i in range(8)]

        KV_PLACE = {(0, 0): 0, (0, 2): 1, (1, 2): 2, (0, 1): 0, (1, 3): 1, (1, 1): 2}

        def kv_of(i4, ch):
            c = KV_PLACE[i4 // 2, ch]
            return bank[4 + i4 % 2 + 2 * (ch % 2)][:, c * P:(c + 1) * P]

        def slot(g):
            return ring[:, (g % RING) * SLOT:(g % RING + 1) * SLOT]

        proj = big[:, 0:TT * D_IN].rearrange("p (t c) -> p t c", t=TT)
        smallw = aux[:, 0:1024]
        la = aux[:, 0:1024].rearrange("p (t c) -> p t c", t=TT)
        decay_exp = aux[:, 1024:3072].rearrange("p (i t w c) -> p i t w c", i=4, t=TT, w=2)
        key_exp = aux[:, 3072:4096].rearrange("p (i t c) -> p i t c", i=4, t=TT)
        gain_rows = aux[0:5 * KD, 4096:4096 + P]
        gqT = aux[:, 4096:4608].rearrange("p (r s) -> p r s", r=2)
        gkT = aux[:, 4608:5120].rearrange("p (r s) -> p r s", r=2)
        key_rest = aux[:, 5120:6144].rearrange("p (i t c) -> p i t c", i=2, t=TT)
        state = aux[:, 6144:7680].rearrange("p (i n c) -> p i n c", i=4, n=3)
        scores = xT_[:, :].rearrange("p (h c) -> p h c", h=GLA_H)
        o_gla = la
        gate_tmp = mix_[:, :].rearrange("p (n t c) -> p n t c", n=2, t=TT)
        small = big[:, TT * D_IN:6144]
        zT = small[:, 0:SEQ]
        gate_up = small[:, 256:768]
        chunk_decay = sb("chunk_decay", 16).rearrange("p (i n) -> p i n", i=4)
        gla_gain = sb("gla_gain", GLA_DV)[:, :]
        qk_gain = small[:, 768:896]
        att_gain = small[:, 896:1408]
        gqa_tmp = xn[:, :, :].rearrange("p t d -> p (t d)")[:, 0:1280].rearrange("p (t h d) -> p t h d", t=TT, d=HD)
        kdup = xn[:, :, :].rearrange("p t d -> p (t d)")[:, 1280:1792].rearrange("p (t k u d) -> p t k u d", t=TT, k=2, u=2)
        gqa_qT = aux[:, 1024:2048].rearrange("p (r s) -> p r s", r=4)
        gqa_kT = aux[:, 2048:2560].rearrange("p (r s) -> p r s", r=2)
        probs = aux[:, 6912:7680].rearrange("p (i c) -> p i c", i=3)
        probsT = aux[:, 5632:6144].rearrange("p (i c) -> p i c", i=2)
        o_att = aux[:, 3072:4096].rearrange("p (t c) -> p t c", t=TT)
        negmax = stat[:, 64:80]
        esum = stat[:, 80:96]
        ersum = stat[:, 96:112]

        cut_at = [0]

        def cut(n):
            cut_at[0] += n
            return big[:, cut_at[0] - n:cut_at[0]]

        w_route = aux[:, 6144:6144 + KD * 72].rearrange("p (k e) -> p k e", k=KD)
        b_route = aux[0:1, 6720:6792]
        logits = cut(2 * 72).rearrange("p (t e) -> p t e", t=TT)
        rt = [cut(128).rearrange("p (t e) -> p t e", t=TT) for _ in range(5)]
        rg = [cut(16).rearrange("p (t e) -> p t e", t=TT) for _ in range(4)]
        rs = [cut(TT) for _ in range(12)]
        picked = cut(2 * NE).rearrange("p (t e) -> p t e", t=TT)
        gate_of = cut(2 * NE).rearrange("p (t e) -> p t e", t=TT)
        place = cut(2 * NE).rearrange("p (t e) -> p t e", t=TT)
        slots_now = cut(TOK)
        rounds_f = cut(8)
        sel = cut(2 * P).rearrange("p (t s) -> p t s", t=TT)
        sel_gate = cut(2 * P).rearrange("p (t s) -> p t s", t=TT)
        sel_gateT = cut(2 * P)
        xg = cut(KD * P).rearrange("p (k s) -> p k s", k=KD)
        eg = cut(2 * P).rearrange("p (i c) -> p i c", i=2)
        hx = cut(2 * P).rearrange("p (i c) -> p i c", i=2)
        hT = cut(2 * P).rearrange("p (i c) -> p i c", i=2)
        y_batch = cut(D)
        assert cut_at[0] <= 6144

        proj2 = big[:, :].rearrange("p (t c) -> p t c", t=TT)
        xn_flat = xn[:, :, :].rearrange("p t d -> p (t d)")
        c_kT = aux[:, 0:2048].rearrange("p (k s) -> p k s", k=KD)
        c_v = aux[:, 4096:6144].rearrange("p (t d) -> p t d", t=TT)
        mem = aux[:, 0:2048].rearrange("p (t d) -> p t d", t=TT)
        memT = aux[:, 2048:4096].rearrange("p (k s) -> p k s", k=KD)
        m_qT = xT_[:, 0:1024].rearrange("p (r s) -> p r s", r=4)
        m_kT = xT_[:, 1024:2048].rearrange("p (r s) -> p r s", r=4)
        r_qT = aux[:, 2048:2560].rearrange("p (r s) -> p r s", r=2)
        r_kT = aux[:, 2560:3072].rearrange("p (r s) -> p r s", r=2)
        probs2 = aux[:, 3072:3584].rearrange("p (i c) -> p i c", i=2)
        m_probs = aux[:, 6912:7680].rearrange("p (i c) -> p i c", i=3)
        probsT2 = aux[:, 3584:4096].rearrange("p (i c) -> p i c", i=2)
        r_scores = aux[:, 6144:7680].rearrange("p (h c) -> p h c", h=RET_H)
        r_square = aux[:, 6144:7168].rearrange("p (t c) -> p t c", t=TT)
        rope_tmp = xn_flat.rearrange("p (n t c) -> p n t c", n=4, t=TT)
        ret_o = xn_flat[:, 0:1024].rearrange("p (t c) -> p t c", t=TT)
        ret_g = xn_flat[:, 1024:2048].rearrange("p (t c) -> p t c", t=TT)
        y = mix
        c_qT = big[:, 0:2048].rearrange("p (k s) -> p k s", k=KD)
        ffT = big[:, 0:KF * SEQ].rearrange("p (k s) -> p k s", k=KF)
        ff_e = xn_flat[:, 0:1024].rearrange("p (i c) -> p i c", i=4)

        x_rows = t_in["x"][0].rearrange("(t p) d -> p t d", p=P)
        mem_rows = t_in["mem_2"][0].rearrange("(t p) d -> p t d", p=P)
        out_rows = out[0].rearrange("(t p) d -> p t d", p=P)

        def chunks(w):
            return w.rearrange("(k p) c -> p k c", p=P)

        used = {g: ("in_mm", 2 * g + 2) for g in range(len(IN_UNITS))}
        for u in range(len(OUT_UNITS)):
            used[len(IN_UNITS) + u] = ("out_mm", TT + u + 1)
        for u in range(len(CK_UNITS)):
            used[len(IN_UNITS) + len(OUT_UNITS) + u] = ("ck_mm", 2 * u + 2)
        G2 = PRE_UNITS + len(MOE_UNITS)
        post = []

        def cols_unit(w, c, signal, value):
            post.append((chunks(w)[:, :, c:c + 512], lambda s: s.rearrange("p (k c) -> p k c", k=KD), signal, value))

        for u in range(2):
            cols_unit(t_in["w_ckv_2"][0], D + 512 * u, "cv_mm", 2 * u + 2)
        for u, c in enumerate(IN2_UNITS):
            cols_unit(t_in["w_in_2"][0], c, "in2_mm", 2 * u + 2)
        for u in range(2):
            cols_unit(t_in["w_out_2"][0], 512 * u, "out2_mm", TT + u + 1)
        for u in range(2):
            cols_unit(t_in["w_cq_2"][0], 512 * u, "cq_mm", 2 * u + 2)
        for u in range(2):
            cols_unit(t_in["w_co_2"][0], 512 * u, "co_mm", TT + u + 1)
        for u in range(N_GU):
            w = t_in["w_gate_up_2"][0]
            post.append(((chunks(w)[:, :, GU_COLS * u:GU_COLS * (u + 1)],
                          chunks(w)[:, :, D_FF + GU_COLS * u:D_FF + GU_COLS * (u + 1)]),
                         lambda s: s.rearrange("p (k w c) -> p k w c", k=KD, w=2), "gu_mm", 2 * u + 2))
        FF_PARTS = [(0, 8), (8, 16), (16, 22)]
        for half in range(2):
            for n, (k0, k1) in enumerate(FF_PARTS):
                post.append((chunks(t_in["w_down_2"][0])[:, k0:k1, 512 * half:512 * half + 512],
                             lambda s, m=k1 - k0: s[:, 0:512 * m].rearrange("p (k c) -> p k c", k=m),
                             "down_mm", 2 * TT))

        def post_wait(eng, u):
            eng.wait_ge(*at(f"w2_in{u % RING}", 32 * (u // RING + 1)))

        block = ctx.enter_context(nc.Block())

        @block.sync
        def _(sp):
            for t in range(TT):
                sp.dma_start(x[:, t, :], x_rows[:, t, :]).then_inc(S("x_in"), 16)
            sp.dma_start(c1[:, :], consts["c1"]).then_inc(S("c1_in"), 16)
            sp.wait_ge(*at("x_in", 16 * TT))
            for g in range(PRE_UNITS):
                if g >= RING:
                    sp.wait_ge(*at(used[g - RING][0], used[g - RING][1]))
                if g < len(IN_UNITS):
                    c, n = IN_UNITS[g]
                    src = chunks(t_in["w_in"][0])[:, :, c:c + n]
                    dst = slot(g)[:, 0:KD * n].rearrange("p (k c) -> p k c", k=KD)
                else:
                    c, n = (OUT_UNITS + CK_UNITS)[g - len(IN_UNITS)]
                    w = t_in["w_out"] if g < len(IN_UNITS) + len(OUT_UNITS) else t_in["w_ckv_2"]
                    src = chunks(w[0])[:, :, c:c + n]
                    dst = slot(g).rearrange("p (k c) -> p k c", k=KD)
                sp.dma_start(dst, src).then_inc(S(f"w1_in{g % RING}"), 16)

            def moe_load(u, expert):
                part, _ = MOE_UNITS[u]
                dst, arrived = slot(PRE_UNITS + u), S(f"moe_in{u % RING}")
                if part == "d":
                    w = t_in["w_down"][0, expert].rearrange("e (k p) c -> p (e k) c", p=P)
                    v = dst.rearrange("p (k c) -> p k c", k=4)
                    sp.dma_start(v[:, 2:4, :], w[:, 2:4, :]).then_inc(arrived, 16)
                    sp.dma_start(v[:, 0:2, :], w[:, 0:2, :]).then_inc(arrived, 16)
                else:
                    k0 = 0 if part == "a" else 4
                    v = dst.rearrange("p (k w c) -> p k w c", k=4, w=2)
                    for n, name in enumerate(("w_gate", "w_up")):
                        w = t_in[name][0, expert].rearrange("e (k p) c -> p (e k) c", p=P)
                        sp.dma_start(v[:, :, n, :], w[:, k0:k0 + 4, :]).then_inc(arrived, 16)

            def moe_slot_free(u, done):
                part, q = MOE_UNITS[u - RING]
                n = done + q + 1 if u >= RING else done - BATCH + q + 1
                sp.wait_ge(*at({"a": "moe_a_used", "b": "moe_gu", "d": "moe_d"}[part], n))

            def experts_of(b, u):
                return bass.ds(b * BATCH + MOE_UNITS[u][1], 1)

            for u in range(RING):
                sp.wait_ge(*at(used[PRE_UNITS + u - RING][0], used[PRE_UNITS + u - RING][1]))
                moe_load(u, bass.ds(MOE_UNITS[u][1], 1))
            with sp.Fori(0, NB - 1) as b:
                for u in range(RING, 2 * RING):
                    moe_slot_free(u, b * BATCH)
                    moe_load(u, experts_of(b, u))
                for u in range(RING):
                    moe_slot_free(u, b * BATCH + BATCH)
                    moe_load(u, experts_of(b + 1, u))
            for u in range(RING, 2 * RING):
                moe_slot_free(u, (NB - 1) * BATCH)
                moe_load(u, experts_of(NB - 1, u))
            sp.wait_ge(*at("rounds_ready", 1))
            rounds = sp.value_load(rounds_i[0:1, 0:1], min_val=1, max_val=MAX_ROUNDS)
            with sp.If(rounds > 1):
                with sp.Fori(1, rounds) as c, sp.Fori(0, NB) as b:
                    for u in range(2 * RING):
                        moe_slot_free(u, c * NE + b * BATCH)
                        moe_load(u, experts_of(b, u))

            for u, (src, view, signal, value) in enumerate(post):
                if u < RING:
                    sp.wait_ge(*at("moe_gu" if u < 4 else "moe_d", rounds * NE))
                else:
                    sp.wait_ge(*at(post[u - RING][2], post[u - RING][3]))
                dst = view(slot(G2 + u))
                if isinstance(src, tuple):
                    for w in range(2):
                        sp.dma_start(dst[:, :, w, :], src[w]).then_inc(S(f"w2_in{u % RING}"), 16)
                else:
                    h = src.shape[1] // 2
                    sp.dma_start(dst[:, 0:h, :], src[:, 0:h, :]).then_inc(S(f"w2_in{u % RING}"), 16)
                    sp.dma_start(dst[:, h:, :], src[:, h:, :]).then_inc(S(f"w2_in{u % RING}"), 16)
            for t in range(TT):
                sp.wait_ge(*at("ffn_x", t + 1))
                sp.dma_start(out_rows[:, t, :], x[:, t, :]).then_inc(S("stored"), 16)
            sp.wait_ge(*at("stored", 16 * TT))

        @block.gpsimd
        def _(pool):
            def load(dst, src, name):
                pool.dma_start(dst, src).then_inc(S(name), 16)

            pool.memset(gate_up[0:33, :], 0.0).then_inc(S("gateup_zero"), 1)
            pool.memset(zT[0:33, :], 1.0).then_inc(S("zT_one"), 1)
            pool.wait_ge(*at("gateup_zero", 1))
            W = GLA_H * GLA_DK
            load(gate_up[0:16, 0:W], t_in["gla_up_fwd"][0], "gateup_in")
            load(gate_up[16:32, W:2 * W], t_in["gla_up_bwd"][0], "gateup_in")
            load(gate_up[32:33, 0:W], t_in["gla_up_fwd_bias"], "gateup_in")
            load(gate_up[32:33, W:2 * W], t_in["gla_up_bwd_bias"], "gateup_in")
            load(gla_mask[:, :], consts["mask"], "mask_in")
            load(gla_gain, t_in["gla_out_gain"][0:1, :].to_broadcast([P, GLA_DV]), "glagain_in")
            load(qk_gain[:, 0:HD], t_in["q_norm_gain"][0:1, :].to_broadcast([P, HD]), "qkgain_in")
            load(qk_gain[:, HD:], t_in["k_norm_gain"][0:1, :].to_broadcast([P, HD]), "qkgain_in")
            load(att_gain, t_in["att_out_gain"][0:1, :].to_broadcast([P, 512]), "attgain_in")
            load(row_gain[:, 0, :], t_in["norm2_gain"][0:1, :].to_broadcast([P, D]), "norm2gain_in")
            load(row_gain[:, 1, :], t_in["final_gain"].rearrange("(o d) -> o d", o=1).to_broadcast([P, D]), "finalgain_in")
            load(c2[:, :], consts["c2"], "c2_in")
            pool_chain = [0]

            def rstd_tile(name, t, col, width=D):
                rstd(name, 1, width, col + t, t + 1)

            def rstd(name, n, width, col, ready):
                pool.wait_ge(*at(f"{name}_ss", ready))
                pool.tensor_scalar(stat[:, col:col + n], stat[:, col:col + n], 1.0 / width, EPS, ALU.mult,
                                   ALU.add).then_inc(S("pool_chain"), 1)
                pool_chain[0] += 1
                pool.wait_ge(*at("pool_chain", pool_chain[0]))
                pool.tensor_tensor(stat[:, col:col + n], stat[:, col:col + n], C1("neghalf", 0, n),
                                   ALU.pow).then_inc(S(f"{name}_rstd"), 1)

            pool.wait_ge(*at("c1_in", 16))
            for t in range(TT):
                rstd_tile("n1", t, 0)
            pool.wait_ge(*at("in_mm", 2 * len(IN_UNITS)))
            pool.memset(xT_[:, :], 0.0).then_inc(S("scores_zero"), 1)
            rstd("gqa", 2 * (GQA_H + GQA_KV), HD, 16, 1)
            rstd("gla", 2 * GLA_H, GLA_DV, 8, 1)
            for t in range(TT):
                rstd_tile("att", t, 2, 512)
            pool.wait_ge(*at("gla_o", TT))
            with nc.allow_non_contiguous_dma(reason="router weights, 72 columns"):
                load(w_route[:, :, 0:NG], chunks(t_in["w_group"][0]), "route_in")
                load(w_route[:, :, NG:], chunks(t_in["w_expert"][0]), "route_in")
            load(b_route[:, 0:NG], t_in["b_group"], "route_in")
            load(b_route[:, NG:], t_in["b_expert"], "route_in")
            pool.wait_ge(*at("mix_n", TT))
            load(mem, mem_rows, "mem_in")
            for t in range(TT):
                rstd_tile("mm", t, 36)
            for t in range(TT):
                rstd_tile("n2", t, 4)
            for t in range(TT):
                rstd_tile("fin", t, 6)
            load(row_gain[:, 0, :], t_in["g_post_mix_2"][0:1, :].to_broadcast([P, D]), "postmix_in")
            for t in range(TT):
                rstd_tile("pm", t, 38)
            pool.wait_ge(*at("x_final", TT))
            load(row_gain[:, 1, :], t_in["g_post_cross_2"][0:1, :].to_broadcast([P, D]), "postcross_in")
            rstd("ret", 2 * RET_H, RET_DV, 40, 1)
            for t in range(TT):
                rstd_tile("om", t, 48)
                rstd_tile("pc", t, 50)
            pool.wait_ge(*at("om_x", TT))
            load(row_gain[:, 0, :], t_in["g_post_ffn_2"][0:1, :].to_broadcast([P, D]), "postffn_in")
            for t in range(TT):
                rstd_tile("oc", t, 52)
                rstd_tile("pf", t, 54)
            for t in range(TT):
                rstd_tile("of", t, 56)

        @block.tensor
        def _(pe):
            def transposes(name, src, t):
                pe.wait_ge(*at(f"{name}_n", t + 1))
                for k in range(KD):
                    i = pe.transpose(bank[4 + 2 * t + k // 4][:, (k % 4) * P:(k % 4 + 1) * P],
                                     src[:, t, k * P:(k + 1) * P], ident)
                i.then_inc(S(f"{name}_tp"), 1)

            def wait_T(name, t):
                pe.wait_ge(*at(f"{name}_Ta", t + 1))
                pe.wait_ge(*at(f"{name}_Tv", t + 1))

            def product(name, lhsT, u, t, w, n=512):
                for k in range(KD):
                    i = pe.matmul(bank[(2 * u + t) % 4][:, 0:n], lhsT[:, k, t * P:(t + 1) * P], w[:, k, :],
                                  start=(k == 0), stop=(k == KD - 1))
                i.then_inc(S(f"{name}_mm"), 1)

            def linear(name, T, lhsT, u, w, n=512):
                for t in range(TT):
                    if u == 0:
                        wait_T(T, t)
                    if u >= 2:
                        pe.wait_ge(*at(f"{name}_ev{t}", u - 1))
                    product(name, lhsT, u, t, w, n)

            def linear_T(name, g, rhsT, j0=0, tiles=slice(0, SEQ)):
                w = slot(g).rearrange("p (k c) -> p k c", k=KD)
                lo, hi = tiles.start, tiles.stop
                for jj in range(2):
                    for m in range(2):
                        for k in range(KD):
                            i = pe.matmul(bank[j0 + jj][:, m * SEQ + lo:m * SEQ + hi],
                                          w[:, k, (2 * jj + m) * P:(2 * jj + m + 1) * P], rhsT[:, k, lo:hi],
                                          start=(k == 0), stop=(k == KD - 1))
                    if hi == SEQ:
                        i.then_inc(S(f"{name}_mm"), 1)

            def attention(pe, name, units, qk, v_of, dv, pr, prT, key_tiles, score_banks, lag, before_third=None):
                NSB, NPR = len(score_banks), pr.shape[1]
                heads = units // TT
                order = [(t, h) for t in range(TT) for h in range(heads)]
                for n in range(units + lag + 1):
                    if n < units:
                        t, h = order[n]
                        if n == 2 and before_third:
                            before_third()
                        if n >= NSB:
                            pe.wait_ge(*at(f"{name}_exp", n - NSB + 1))
                        parts = qk(h, t)
                        parts = parts if isinstance(parts, list) else [parts]
                        w = key_tiles(t) * P
                        for m, (a, b) in enumerate(parts):
                            i = pe.matmul(bank[score_banks[n % NSB]][:, 0:w], a, b[:, 0:w], start=(m == 0), stop=(m == len(parts) - 1))
                        i.then_inc(S(f"{name}_sc"), 1)
                    if lag <= n < units + lag:
                        m = n - lag
                        pe.wait_ge(*at(f"{name}_exp", m + 1))
                        if m >= 2:
                            pe.wait_ge(*at(f"{name}_PT", m - 1))
                        for k in range(key_tiles(order[m][0])):
                            i = pe.transpose(bank[6 + m % 2][:, k * P:(k + 1) * P], pr[:, m % NPR, k * P:(k + 1) * P], ident)
                        i.then_inc(S(f"{name}_ptp"), 1)
                    if n >= lag + 1:
                        m = n - lag - 1
                        t, h = order[m]
                        pe.wait_ge(*at(f"{name}_PT", m + 1))
                        kt = key_tiles(t)
                        per = 512 // dv
                        b, c = (4 + t, h) if heads <= per else (None, None)
                        if heads > per:
                            b, c = (4 if t == 0 else 0) + h // per, h % per
                        for k in range(kt):
                            i = pe.matmul(bank[b][:, c * dv:(c + 1) * dv], prT[:, m % 2, k * P:(k + 1) * P], v_of(h, t, k),
                                          start=(k == 0), stop=(k == kt - 1))
                        i.then_inc(S(f"{name}_pv"), 1)

            pe.wait_ge(*at("c1_in", 16))
            pe.wait_ge(*at("colgain_in", 80))
            pe.transpose(bank[6][:, 0:5 * KD], gain_rows, ident[0:5 * KD, 0:5 * KD]).then_inc(S("colgain_tp"), 1)
            for t in range(TT):
                transposes("n1", xn, t)
            for u, (c, n) in enumerate(IN_UNITS):
                pe.wait_ge(*at(f"w1_in{u}", 16))
                linear("in", "n1", xT, u, slot(u)[:, 0:KD * n].rearrange("p (k c) -> p k c", k=KD), n)
                if u == 1:
                    for t in range(TT):
                        pe.wait_ge(*at(f"in_ev{t}", 1))
                    for t in range(TT):
                        i = pe.transpose(bank[4][0:32, t * P:(t + 1) * P], proj[:, t, C_Z:C_Z + 32], ident)
                    i.then_inc(S("zT_tp"), 1)
                if u == 2:
                    pe.wait_ge(*at("zT_ev", 1))
                    pe.wait_ge(*at("gateup_in", 64))
                    for t in range(TT):
                        pe.matmul(bank[6 + t][:, :], zT[0:33, t * P:(t + 1) * P], gate_up[0:33, :], start=True,
                                  stop=True).then_inc(S("gate_mm"), 1)
                if u == 3:
                    for t in range(TT):
                        pe.wait_ge(*at(f"in_ev{t}", 2))
                    for w, c0 in enumerate((C_GQ, C_GK)):
                        for r in range(2):
                            for t in range(TT):
                                i = pe.transpose(bank[4 + w][:, r * SEQ + t * P:r * SEQ + (t + 1) * P],
                                                 proj[:, t, c0 + r * P:c0 + (r + 1) * P], ident)
                        i.then_inc(S("gqk_tp"), 1)
            for i4 in range(4):
                di, r = i4 // 2, i4 % 2
                if i4 == 0:
                    pe.wait_ge(*at("la", 2))
                    pe.wait_ge(*at("gqkT", 2))
                if i4 >= 2:
                    pe.wait_ge(*at("sum_exp", i4 - 1))
                for t in range(TT):
                    i = pe.matmul(bank[4 + i4 % 2][:, t * SEQ:(t + 1) * SEQ],
                                  la[:, t, di * SEQ + r * P:di * SEQ + (r + 1) * P],
                                  C1("cum_f" if di == 0 else "cum_b"), start=True, stop=True)
                i.then_inc(S("sum_mm"), 1)
            for di in range(2):
                for t in range(TT):
                    i = pe.matmul(bank[6 + di][:, t * SEQ:(t + 1) * SEQ], C1("rest_f" if di == 0 else "rest_b"),
                                  la[:, t, di * SEQ:(di + 1) * SEQ], start=True, stop=True)
                i.then_inc(S("rest_mm"), 1)
            for h in range(GLA_H):
                r, o = h // 2, 64 * (h % 2)
                if h == 0:
                    for t in range(TT):
                        pe.wait_ge(*at(f"in_ev{t}", len(IN_UNITS)))
                for di in range(2):
                    pe.wait_ge(*at("gla_qk", 2 * di + r + 1))
                    for t in range(TT):
                        i = pe.matmul(bank[h][:, (2 * di + t) * P:(2 * di + t + 1) * P],
                                      key_exp[o:o + 64, 2 * di + r, t, :], decay_exp[o:o + 64, 2 * di + r, t, 0, :],
                                      start=True, stop=True)
                i.then_inc(S("gla_sc"), 1)
            for i4 in range(4):
                di, r = i4 // 2, i4 % 2
                pe.wait_ge(*at("key_rest", di + 1))
                if i4 == 0:
                    pe.wait_ge(*at("sum_exp", 4))
                    pe.wait_ge(*at("key_rest", 2))
                for n in range(3):
                    ch = n if di == 0 else 3 - n
                    t, o = ch // 2, 64 * (ch % 2)
                    for hh in range(2):
                        i = pe.matmul(kv_of(i4, ch)[64 * hh:64 * hh + 64, :],
                                      key_rest[o:o + 64, di, t, r * P + 64 * hh:r * P + 64 * hh + 64],
                                      proj[o:o + 64, t, C_GV + (2 * r + hh) * P:C_GV + (2 * r + hh + 1) * P],
                                      start=True, stop=True)
                i.then_inc(S("gla_kv"), 1)
            pe.wait_ge(*at("gla_masked", GLA_H))
            pe.wait_ge(*at("gla_state", 4))
            for t in range(TT):
                for h in range(GLA_H):
                    r, o = h // 2, 64 * (h % 2)
                    b = bank[2 * (h % 2) + t]
                    dst = b[:, r * P:(r + 1) * P]
                    for di in range(2):
                        pe.matmul(dst, scores[:, h, (2 * di + t) * P:(2 * di + t + 1) * P],
                                  proj[:, t, C_GV + h * P:C_GV + (h + 1) * P], start=(di == 0), stop=(di == 1))
                    parts = [(di, ch) for ch in (2 * t, 2 * t + 1) for di in range(2)
                             if (ch > 0 if di == 0 else ch < 3)]
                    for di, ch in parts:
                        cc = 64 * (ch % 2)
                        n = ch - 1 if di == 0 else 2 - ch
                        i = pe.matmul(b[cc:cc + 64, r * P:(r + 1) * P],
                                      decay_exp[o:o + 64, 2 * di + r, t, 1, cc:cc + 64],
                                      state[o:o + 64, 2 * di + r, n, :], start=False, stop=True,
                                      skip_group_check=True)
                i.then_inc(S("gla_o"), 1)
            pe.wait_ge(*at("gqa_qk", 1))
            for t in range(TT):
                for r in range(4):
                    i = pe.transpose(bank[4 + r // 2][:, (r % 2) * SEQ + t * P:(r % 2) * SEQ + (t + 1) * P],
                                     proj[:, t, C_AQ + r * P:C_AQ + (r + 1) * P], ident)
            for t in range(TT):
                for r in range(2):
                    i = pe.transpose(bank[6][:, r * SEQ + t * P:r * SEQ + (t + 1) * P],
                                     kdup[:, t, r, :, :].rearrange("p u d -> p (u d)"), ident)
            i.then_inc(S("gqa_tp"), 1)
            pe.wait_ge(*at("gqa_T", 3))
            attention(pe, "gqa", 16, lambda h, t: (gqa_qT[64 * (h % 2):64 * (h % 2) + 64, h // 2, t * P:(t + 1) * P],
                                                   gqa_kT[64 * (h % 2):64 * (h % 2) + 64, h // 4, :]),
                      lambda h, t, k: proj[:, k, C_AV + (h // 4) * HD:C_AV + (h // 4 + 1) * HD], HD,
                      probs, probsT, lambda t: TT, (0, 1, 2, 3), 3)
            for t in range(TT):
                transposes("mix", mix, t)
            for t in range(TT):
                wait_T("mix", t)
                for u in range(2):
                    g = len(IN_UNITS) + u
                    if t == 0:
                        pe.wait_ge(*at(f"w1_in{g % RING}", 16 * (g // RING + 1)))
                    product("out", xT, u, t, slot(g).rearrange("p (k c) -> p k c", k=KD))
                if t == 0:
                    wait_T("mix", 1)
                    for tm in range(TT):
                        transposes("mm", mem, tm)
            for t in range(TT):
                wait_T("mm", t)

            def cross_keys(j):
                g = len(IN_UNITS) + len(OUT_UNITS) + j // 2
                if j % 2 == 0:
                    pe.wait_ge(*at(f"w1_in{g % RING}", 16 * (g // RING + 1)))
                w = slot(g).rearrange("p (k c) -> p k c", k=KD)
                for m in range(2):
                    for k in range(KD):
                        i = pe.matmul(bank[CK_BANKS[j]][:, m * SEQ:(m + 1) * SEQ],
                                      w[:, k, (2 * (j % 2) + m) * P:(2 * (j % 2) + m + 1) * P], memT[:, k, :],
                                      start=(k == 0), stop=(k == KD - 1))
                i.then_inc(S("ck_mm"), 1)

            pe.wait_ge(*at("out_ev0", 2))
            cross_keys(0)
            for t in range(TT):
                transposes("n2", xn, t)
            pe.wait_ge(*at("route_in", 64))
            for t in range(TT):
                wait_T("n2", t)
                pe.matmul(bank[t][:, 0:72], C1("ones")[0:1, :], b_route, start=True, stop=False)
                for k in range(KD):
                    i = pe.matmul(bank[t][:, 0:72], xT[:, k, t * P:(t + 1) * P], w_route[:, k, :], start=False,
                                  stop=(k == KD - 1))
            i.then_inc(S("route_mm"), 1)
            cross_keys(1)
            cross_keys(2)
            pe.wait_ge(*at("picked", 1))
            pe.matmul(bank[3][:, 0:NE], C1("before"), picked[:, 0, :], start=True, stop=True)
            pe.matmul(bank[3][:, NE:2 * NE], C1("before"), picked[:, 1, :], start=True, stop=False)
            pe.matmul(bank[3][:, NE:2 * NE], C1("ones"), picked[:, 0, :], start=False, stop=True)
            pe.matmul(bank[3][:, 2 * NE:3 * NE], C1("ones"), picked[:, 0, :], start=True, stop=False)
            pe.matmul(bank[3][:, 2 * NE:3 * NE], C1("ones"), picked[:, 1, :], start=False, stop=True
                      ).then_inc(S("place_mm"), 1)
            cross_keys(3)
            for t in range(TT):
                pe.wait_ge(*at(f"ck_ev{t}", 2))

            pe.wait_ge(*at("rounds_ready", 1))
            rounds = pe.value_load(rounds_i[0:1, 0:1], min_val=1, max_val=MAX_ROUNDS)
            with pe.Fori(0, rounds) as c, pe.Fori(0, NB) as b:
                it = c * NB + b

                def arrive(part, q):
                    u = MOE_UNITS.index((part, q))
                    pe.wait_ge(*at(f"moe_in{u % RING}", it * 64 + 32 * (u // RING + 1)))
                    return slot(PRE_UNITS + u)

                def gate_up_half(part, q):
                    w = arrive(part, q).rearrange("p (k w c) -> p k w c", k=4, w=2)
                    for k in range(4):
                        for j in range(4):
                            i = pe.matmul(bank[q % 2][TOK * j:TOK * (j + 1), 0:SEQ],
                                          xg[:, k + (0 if part == "a" else 4), TOK * q:TOK * (q + 1)],
                                          w[:, k, :, j * P:(j + 1) * P], start=(part == "a" and k == 0),
                                          stop=(part == "b" and k == 3), tile_position=(0, TOK * j))
                    i.then_inc(S("moe_a_used" if part == "a" else "moe_gu"), 1)

                def h_transpose(q):
                    pe.wait_ge(*at("moe_h", it * BATCH + q + 1))
                    pe.transpose(bank[4][:, 0:P], hx[:, q % 2, :], ident).then_inc(S("moe_hT_tp"), 1)

                def down(q):
                    w = arrive("d", q).rearrange("p (k c) -> p k c", k=4)
                    pe.wait_ge(*at("moe_hT", it * BATCH + q + 1))
                    for half in range(2):
                        for j in range(4):
                            i = pe.matmul(bank[6 + half][TOK * q:TOK * (q + 1), :], hT[:, q % 2, TOK * j:TOK * (j + 1)],
                                          w[:, j, half * 512:(half + 1) * 512], start=(j == 0), stop=(j == 3),
                                          tile_position=(0, TOK * q))
                    i.then_inc(S("moe_d"), 1)

                pe.wait_ge(*at("moe_sel", it + 1))
                for t in range(TT):
                    i = pe.transpose(bank[5][:, t * P:(t + 1) * P], sel_gate[:, t, :], ident)
                i.then_inc(S("moe_selT_tp"), 1)
                pe.wait_ge(*at("moe_xadd", it * 4 + 1))
                for k in range(KD):
                    for t in range(TT):
                        i = pe.matmul(bank[2 + k // 4][:, (k % 4) * P:(k % 4 + 1) * P], xn[:, t, k * P:(k + 1) * P],
                                      sel[:, t, :], start=(t == 0), stop=(t == TT - 1))
                    if k % 4 == 3:
                        i.then_inc(S("moe_xg_mm"), 1)
                pe.wait_ge(*at("moe_xg_a", it + 1))
                pe.wait_ge(*at("moe_xg_v", it + 1))
                gate_up_half("a", 0)
                gate_up_half("b", 0)
                for q in range(1, BATCH):
                    gate_up_half("a", q)
                    h_transpose(q - 1)
                    gate_up_half("b", q)
                    down(q - 1)
                h_transpose(BATCH - 1)
                down(BATCH - 1)
                pe.wait_ge(*at("moe_selT", it + 1))
                for half in range(2):
                    pe.wait_ge(*at("moe_y_a" if half == 0 else "moe_y_v", it + 1))
                    for t in range(TT):
                        n = 2 * half + t
                        if n >= 2:
                            pe.wait_ge(*at("moe_xadd", it * 4 + n))
                        pe.matmul(bank[2 + n % 2][:, :], sel_gateT[:, t * P:(t + 1) * P],
                                  y_batch[:, half * 512:(half + 1) * 512], start=True, stop=True
                                  ).then_inc(S("moe_cmb"), 1)
            def unit_of(g):
                return slot(G2 + g).rearrange("p (k c) -> p k c", k=KD)

            def post_linear(name, T, lhsT, u, g):
                post_wait(pe, g)
                linear(name, T, lhsT, u, unit_of(g))

            def out_linear(name, T, g, next_T):
                for t in range(TT):
                    wait_T(T, t)
                    for u in range(2):
                        if t == 0:
                            post_wait(pe, g + u)
                        if (t, u) == (1, 1):
                            transposes(next_T, xn, 0)
                        product(name, xT, u, t, unit_of(g + u))

            def emptied(name, n):
                for t in range(TT):
                    pe.wait_ge(*at(f"{name}_ev{t}", n))

            pe.wait_ge(*at("moe_x", 1))
            for u in range(2):
                post_linear("cv", "mm", memT, u, u)
            for t in range(TT):
                transposes("pm", xn, t)
            emptied("cv", 2)
            for u in range(6):
                if u == 5:
                    emptied("in2", 5)
                    pe.wait_ge(*at("rope", 1))
                    for w, c0 in enumerate((C_MQ, C_MK)):
                        for r in range(4):
                            for t in range(TT):
                                i = pe.transpose(bank[4 + 2 * w + r // 2][:, (r % 2) * SEQ + t * P:(r % 2) * SEQ + (t + 1) * P],
                                                 proj2[:, t, c0 + r * P:c0 + (r + 1) * P], ident)
                            if r % 2 == 1:
                                i.then_inc(S("m_tp"), 1)
                    pe.wait_ge(*at("rope", 2))
                    for w, c0 in enumerate((C_RQ, C_RK)):
                        for r in range(2):
                            for t in range(TT):
                                i = pe.transpose(bank[w][:, r * SEQ + t * P:r * SEQ + (t + 1) * P],
                                                 proj2[:, t, c0 + r * P:c0 + (r + 1) * P], ident)
                        i.then_inc(S("r_tp"), 1)
                post_linear("in2", "pm", xT, u, 2 + u)
            emptied("in2", 6)
            pe.wait_ge(*at("r_T", 2))
            for h in range(RET_H):
                r, o = h // 2, 64 * (h % 2)
                pe.matmul(bank[h][:, 0:SEQ], r_kT[o:o + 64, r, 0:P], r_qT[o:o + 64, r, :], start=True, stop=True)
                pe.matmul(bank[h][:, SEQ:SEQ + P], r_kT[o:o + 64, r, P:SEQ], r_qT[o:o + 64, r, P:SEQ], start=True,
                          stop=True).then_inc(S("ret_sc"), 1)
            pe.wait_ge(*at("ret_decayed", RET_H))
            for t in range(TT):
                for h in range(RET_H):
                    for k in range(t + 1):
                        c = t * P if k == 0 else SEQ
                        i = pe.matmul(bank[t][:, h * P:(h + 1) * P], r_scores[:, h, c:c + P],
                                      proj2[:, k, C_RV + h * P:C_RV + (h + 1) * P], start=(k == 0), stop=(k == t))
                i.then_inc(S("ret_o"), 1)
            pe.wait_ge(*at("m_T", 4))
            attention(pe, "moba", 16, lambda h, t: (m_qT[64 * (h % 2):64 * (h % 2) + 64, h // 2, t * P:(t + 1) * P],
                                                    m_kT[64 * (h % 2):64 * (h % 2) + 64, h // 2, :]),
                      lambda h, t, k: proj2[:, k, C_MV + h * HD:C_MV + (h + 1) * HD], HD, m_probs, probsT2,
                      lambda t: t + 1, (2, 3, 0, 1), 2, lambda: pe.wait_ge(*at("ret_oc", TT)))
            pe.wait_ge(*at("mix2_n", TT))
            for t in range(TT):
                transposes("mix2", mix, t)
            out_linear("out2", "mix2", 8, "pc")
            emptied("out2", 2)
            for t in range(TT):
                wait_T("pc", t)
                for u in range(2):
                    if t == 0:
                        post_wait(pe, 10 + u)
                    linear_T("cq", G2 + 10 + u, xT, 2 * u, slice(t * P, (t + 1) * P))
                    if (t, u) == (0, 0):
                        transposes("pc", xn, 1)
            emptied("cq", 2)
            attention(pe, "cross", 8, lambda h, t: [(c_qT[:, 2 * h + m, t * P:(t + 1) * P], c_kT[:, 2 * h + m, :])
                                                    for m in range(2)],
                      lambda h, t, k: c_v[:, k, h * CROSS_D:(h + 1) * CROSS_D], CROSS_D, probs2, probsT2,
                      lambda t: TT, (2, 3), 1)
            for t in range(TT):
                transposes("cmix", mix, t)
            out_linear("co", "cmix", 12, "pf")
            emptied("co", 2)

            def hidden(j, lo, hi):
                w = slot(G2 + 14 + j // 2).rearrange("p (k w c) -> p k w c", k=KD, w=2)
                for gu in range(2):
                    for k in range(KD):
                        i = pe.matmul(bank[j % 4][:, gu * SEQ + lo:gu * SEQ + hi],
                                      w[:, k, gu, (j % 2) * P:(j % 2 + 1) * P],
                                      xT[:, k, lo:hi], start=(k == 0), stop=(k == KD - 1))
                if hi == SEQ:
                    i.then_inc(S("gu_mm"), 1)

            wait_T("pf", 0)
            for j in range(4):
                if j % 2 == 0:
                    post_wait(pe, 14 + j // 2)
                hidden(j, 0, P)
                if j == 1:
                    transposes("pf", xn, 1)
            wait_T("pf", 1)
            for j in range(4):
                hidden(j, P, SEQ)
            for j in range(4, KF):
                if j % 2 == 0:
                    post_wait(pe, 14 + j // 2)
                pe.wait_ge(*at("ff_h", j - 3))
                hidden(j, 0, SEQ)
            for t in range(TT):
                for half in range(2):
                    for n, (k0, k1) in enumerate(FF_PARTS):
                        g = 14 + N_GU + 3 * half + n
                        if t == 0:
                            post_wait(pe, g)
                        if (t, half) == (0, 0):
                            pe.wait_ge(*at("ff_h", k1))
                        w = slot(G2 + g)[:, 0:512 * (k1 - k0)].rearrange("p (k c) -> p k c", k=k1 - k0)
                        for k in range(k0, k1):
                            i = pe.matmul(bank[4 + 2 * half + t][:, :], ffT[:, k, t * P:(t + 1) * P], w[:, k - k0, :],
                                          start=(k == 0), stop=(k == KF - 1))
                    i.then_inc(S("down_mm"), 1)


        @block.scalar
        def _(act):
            A = nc.scalar.activation
            act_chain = [0]

            def link(i):
                i.then_inc(S("act_chain"), 1)
                act_chain[0] += 1
                act.wait_ge(*at("act_chain", act_chain[0]))

            def squares(name, src, col, junk, ready):
                for t in range(TT):
                    ready(t)
                    square(name, src, col, junk, t)

            def square(name, src, col, junk, t):
                A(junk[:, t, :], src[:, t, :], ACT.Square, accum_out=stat[:, col + t:col + t + 1]
                  ).then_inc(S(f"{name}_ss"), 1)

            def evac_T(name, gain=None, dst=xT, tiles=range(TT)):
                for t in tiles:
                    act.wait_ge(*at(f"{name}_tp", t + 1))
                    src = bank[4 + 2 * t]
                    if gain is None:
                        i = A(dst[:, 0:4, t * P:(t + 1) * P], src[:, :].rearrange("p (k s) -> p k s", k=4), ACT.Copy)
                    else:
                        for k in range(4):
                            i = A(dst[:, k, t * P:(t + 1) * P], src[:, k * P:(k + 1) * P], ACT.Copy,
                                  scale=col_gain[:, gain, k:k + 1])
                    i.then_inc(S(f"{name}_Ta"), 1)

            def softmax(name, units, pr, key_tiles, score_banks, tile0_out=None):
                heads, NSB, NPR = units // TT, len(score_banks), pr.shape[1]
                for n in range(units):
                    act.wait_ge(*at(f"{name}_nm", n + 1))
                    if n >= NPR:
                        act.wait_ge(*at(f"{name}_ptp", n - NPR + 1))
                    if n == heads + 5 and tile0_out:
                        tile0_out()
                    w = key_tiles(n // heads) * P
                    src = bank[score_banks[n % NSB]][:, 0:w] if name != "moba" else pr[:, n % NPR, 0:w]
                    A(pr[:, n % NPR, 0:w], src, ACT.Exp, bias=negmax[:, n:n + 1],
                      accum_out=esum[:, n:n + 1]).then_inc(S(f"{name}_exp"), 1)

            for r, name in enumerate(("norm1_gain", "g_pre_mix_2", "g_mem_2", "g_pre_cross_2", "g_pre_ffn_2")):
                act.dma_start(gain_rows[KD * r:KD * (r + 1), :], t_in[name][0].rearrange("(k p) -> k p", p=P)
                              ).then_inc(S("colgain_in"), 16)
            act.wait_ge(*at("x_in", 16 * TT))
            squares("n1", x, 0, mix, lambda t: None)
            act.wait_ge(*at("colgain", 1))
            evac_T("n1", 0)

            def in_evac(u):
                c, n = IN_UNITS[u]
                act.wait_ge(*at("in_mm", 2 * u + 1))
                A(proj[:, 0, c:c + n], bank[(2 * u) % 4][:, 0:n], ACT.Copy).then_inc(S("in_ev0"), 1)

            for u in range(3):
                in_evac(u)
            for t in range(TT):
                act.wait_ge(*at("gate_mm", t + 1))
                link(A(gate_tmp[:, 0, t, :], bank[6 + t][:, :], ACT.Abs))
                link(A(gate_tmp[:, 1, t, :], gate_tmp[:, 0, t, :], ACT.Exp, scale=-1.0))
                A(gate_tmp[:, 0, t, :], gate_tmp[:, 1, t, :], ACT.Ln, bias=1.0).then_inc(S("gate_ln"), 1)
            in_evac(3)
            act.wait_ge(*at("gqk_tp", 1))
            A(gqT[:, :, :].rearrange("p r s -> p (r s)"), bank[4][:, :], ACT.Copy, scale=GLA_DK ** -0.5
              ).then_inc(S("gqkT"), 1)
            in_evac(4)
            for i4 in range(4):
                act.wait_ge(*at("sum_mm", i4 + 1))
                b = bank[4 + i4 % 2][:, :]
                A(decay_exp[:, i4, :, :, :].rearrange("p t w c -> p (t w c)"), b, ACT.Exp, scale=1.0 / GATE_NORM)
                A(key_exp[:, i4, :, :], b.rearrange("p (t w c) -> p t w c", t=TT, w=2)[:, :, 0, :], ACT.Exp,
                  scale=-1.0 / GATE_NORM).then_inc(S("sum_exp"), 1)
            for di in range(2):
                act.wait_ge(*at("rest_mm", di + 1))
                A(key_rest[:, di, :, :].rearrange("p t c -> p (t c)"), bank[6 + di][:, :], ACT.Exp,
                  scale=1.0 / GATE_NORM).then_inc(S("rest_exp"), 1)
            act.wait_ge(*at("in_ev0", 4))
            act.wait_ge(*at("in_ev1", 4))
            for t in range(TT):
                A(gqa_tmp[:, t, :, :].rearrange("p h d -> p (h d)"), proj[:, t, C_AQ:C_AV], ACT.Square
                  ).then_inc(S("gqa_sq"), 1)
            act.wait_ge(*at("in_ev0", 5))
            act.wait_ge(*at("in_ev1", 5))
            A(gate_tmp[:, 0, :, :], proj[:, :, C_GG:C_GG + 512], ACT.Silu).then_inc(S("gg_silu"), 1)
            for t in range(TT):
                act.wait_ge(*at("gla_o", t + 1))
                for odd in range(2):
                    src = bank[2 * odd + t][:, 0:2 * P].rearrange("p (r d) -> p r d", r=2)
                    for dst, f, name in ((o_gla[:, t, :], ACT.Copy, "gla_oc"), (gate_tmp[:, 1, t, :], ACT.Square, "gla_sq")):
                        A(dst.rearrange("p (r o d) -> p r o d", r=2, o=2)[:, :, odd, :], src, f).then_inc(S(name), 1)
            act.wait_ge(*at("gqa_tp", 1))
            for r in range(2):
                A(gqa_qT[:, 2 * r:2 * r + 2, :].rearrange("p r s -> p (r s)"), bank[4 + r][:, :], ACT.Copy,
                  scale=HD ** -0.5).then_inc(S("gqa_T"), 1)

            def att_squares(t):
                act.wait_ge(*at("att_o", t + 1))
                square("att", o_att, 2, xn[:, :, 0:512], t)

            softmax("gqa", 16, probs, lambda t: TT, (0, 1, 2, 3), lambda: att_squares(0))
            att_squares(1)
            evac_T("mix")
            squares("mm", mem, 36, c_v, lambda t: act.wait_ge(*at("mem_in", 16)))
            evac_T("mm", 2, memT)
            squares("n2", x, 4, mix, lambda t: act.wait_ge(*at(f"out_ev{t}", 2)))

            def keys(j):
                act.wait_ge(*at("ck_mm", j + 1))
                A(c_kT[:, 2 * j:2 * j + 2, :].rearrange("p k s -> p (k s)"), bank[CK_BANKS[j]][:, :], ACT.Copy
                  ).then_inc(S(f"ck_ev{j % 2}"), 1)

            keys(0)
            evac_T("n2")
            act.wait_ge(*at("route_d", 1))
            A(rg[1], rg[0], ACT.Exp).then_inc(S("route_e"), 1)
            act.wait_ge(*at("route_d", 2))
            A(rs[6], rs[5], ACT.Exp).then_inc(S("route_e"), 1)
            for j in range(1, 4):
                keys(j)

            act.wait_ge(*at("rounds_ready", 1))
            rounds = act.value_load(rounds_i[0:1, 0:1], min_val=1, max_val=MAX_ROUNDS)
            with act.Fori(0, rounds) as c, act.Fori(0, NB) as b:
                it = c * NB + b
                act.wait_ge(*at("moe_selT_tp", it + 1))
                A(sel_gateT, bank[5][:, 0:SEQ], ACT.Copy).then_inc(S("moe_selT"), 1)
                act.wait_ge(*at("moe_xg_mm", it * 2 + 1))
                A(xg[:, 0:4, :].rearrange("p k s -> p (k s)"), bank[2][:, :], ACT.Copy).then_inc(S("moe_xg_a"), 1)
                for q in range(BATCH):
                    act.wait_ge(*at("moe_gu", it * BATCH + q + 1))
                    A(eg[:, q % 2, :], bank[q % 2][:, 0:P], ACT.Silu).then_inc(S("moe_e"), 1)
                    act.wait_ge(*at("moe_hT_tp", it * BATCH + q + 1))
                    A(hT[:, q % 2, :], bank[4][:, 0:P], ACT.Copy).then_inc(S("moe_hT"), 1)
                act.wait_ge(*at("moe_d", it * BATCH + BATCH))
                A(y_batch[:, 0:512], bank[6][:, :], ACT.Copy).then_inc(S("moe_y_a"), 1)
            squares("fin", x, 6, mix, lambda t: act.wait_ge(*at("moe_x", 1)))
            def evac_even(name, n, dst_of, bank_of, scale=1.0):
                for u in range(n):
                    act.wait_ge(*at(f"{name}_mm", 2 * u + 1))
                    A(dst_of(u), bank_of(u), ACT.Copy, scale=scale).then_inc(S(f"{name}_ev0"), 1)

            def two_chunks(dst, j):
                return dst[:, 2 * j:2 * j + 2, :].rearrange("p k s -> p (k s)")

            squares("pm", x, 38, mix, lambda t: act.wait_ge(*at("x_final", t + 1)))
            evac_even("cv", 2, lambda u: c_v[:, 0, 512 * u:512 * (u + 1)], lambda u: bank[(2 * u) % 4][:, :])
            evac_T("pm", 1)
            evac_even("in2", 5, lambda u: proj2[:, 0, IN2_UNITS[u]:IN2_UNITS[u] + 512], lambda u: bank[(2 * u) % 4][:, :])
            act.wait_ge(*at("r_tp", 1))
            A(two_chunks(r_qT, 0), bank[0][:, :], ACT.Copy).then_inc(S("r_T"), 1)
            act.wait_ge(*at("in2_mm", 11))
            A(proj2[:, 0, IN2_UNITS[5]:IN2_UNITS[5] + 512], bank[2][:, :], ACT.Copy).then_inc(S("in2_ev0"), 1)
            for r in range(2):
                act.wait_ge(*at("m_tp", r + 1))
                if r == 0:
                    act.wait_ge(*at("in2_mm", 12))
                A(two_chunks(m_qT, r), bank[4 + r][:, :], ACT.Copy, scale=HD ** -0.5).then_inc(S("m_T"), 1)
            act.wait_ge(*at("rope", 2))
            act.wait_ge(*at("in2_ev0", 6))
            act.wait_ge(*at("in2_ev1", 6))
            A(ret_g, proj2[:, :, C_RG:C_RG + 512], ACT.Silu).then_inc(S("rg_silu"), 1)
            act.wait_ge(*at("ret_o", TT))
            for t in range(TT):
                A(r_square[:, t, :], bank[t][:, :], ACT.Square).then_inc(S("ret_sq"), 1)
            for t in range(TT):
                A(ret_o[:, t, :], bank[t][:, :], ACT.Copy).then_inc(S("ret_oc"), 1)
            softmax("moba", 16, m_probs, lambda t: t + 1, (2, 3, 0, 1))
            evac_T("mix2")

            def y_half(name, t):
                for u in range(2):
                    act.wait_ge(*at(f"{name}_mm", 2 * t + u + 1))
                    A(y[:, t, 512 * u:512 * (u + 1)], bank_y(name, u, t)[:, :], ACT.Copy).then_inc(S(f"{name}_ev{t}"), 1)

            def bank_y(name, u, t):
                return bank[4 + 2 * u + t] if name == "down" else bank[(2 * u + t) % 4]

            def y_square(name, of, col, t):
                act.wait_ge(*at(f"{name}_ev{t}", 2))
                square(of, y, col, xn, t)

            def y_and_next(name, of, col, nx, next_col, gain):
                y_half(name, 0)
                for t in range(TT):
                    y_square(name, of, col, t)
                    act.wait_ge(*at(f"{of}_x", t + 1))
                    square(nx, x, next_col, mix, t)
                    evac_T(nx, gain, tiles=(t,))

            y_and_next("out2", "om", 48, "pc", 50, 3)
            evac_even("cq", 2, lambda u: two_chunks(c_qT, 2 * u), lambda u: bank[2 * u][:, :], CROSS_D ** -0.5)
            softmax("cross", 8, probs2, lambda t: TT, (2, 3))
            evac_T("cmix")
            y_and_next("co", "oc", 52, "pf", 54, 4)
            for j in range(KF):
                act.wait_ge(*at("gu_mm", j + 1))
                if j >= 4:
                    act.wait_ge(*at("ff_h", j - 3))
                A(ff_e[:, j % 4, :], bank[j % 4][:, 0:SEQ], ACT.Silu).then_inc(S("ff_silu"), 1)
            y_half("down", 0)
            for t in range(TT):
                y_square("down", "of", 56, t)

        @block.vector
        def _(dve):
            V = nc.vector
            dve_chain = [0]

            def link(i):
                i.then_inc(S("dve_chain"), 1)
                dve_chain[0] += 1
                dve.wait_ge(*at("dve_chain", dve_chain[0]))

            def scaled(name, src, col, gain=None, dst=xn, signal=None, tiles=range(TT)):
                for t in tiles:
                    dve.wait_ge(*at(f"{name}_rstd", t + 1))
                    r = stat[:, col + t:col + t + 1]
                    if gain is None:
                        i = V.tensor_scalar(dst[:, t, :], src[:, t, :], r, None, ALU.mult)
                    else:
                        i = V.scalar_tensor_tensor(dst[:, t, :], src[:, t, :], r, gain, ALU.mult, ALU.mult)
                    i.then_inc(S(signal or f"{name}_n"), 1)

            def evac_T(name, gain=None, dst=xT, tiles=range(TT)):
                for t in tiles:
                    dve.wait_ge(*at(f"{name}_tp", t + 1))
                    src = bank[5 + 2 * t]
                    if gain is None:
                        i = V.tensor_copy(dst[:, 4:8, t * P:(t + 1) * P], src[:, :].rearrange("p (k s) -> p k s", k=4))
                    else:
                        i = V.tensor_tensor(dst[:, 4:8, t * P:(t + 1) * P], src[:, :].rearrange("p (k s) -> p k s", k=4),
                                            col_gain[:, gain, 4:8].unsqueeze(2).to_broadcast([P, 4, P]), ALU.mult)
                    i.then_inc(S(f"{name}_Tv"), 1)

            def attend(name, units, prT, key_tiles, maximum, lag, output):
                heads = units // TT
                for n in range(units + lag):
                    if n < units:
                        dve.wait_ge(*at(f"{name}_sc", n + 1))
                        maximum(n)
                    if n == heads + lag + 1:
                        output(0)
                    if n >= lag:
                        m = n - lag
                        dve.wait_ge(*at(f"{name}_ptp", m + 1))
                        if m >= 2:
                            dve.wait_ge(*at(f"{name}_pv", m - 1))
                        w = key_tiles(m // heads) * P
                        V.tensor_copy(prT[:, m % 2, 0:w], bank[6 + m % 2][:, 0:w]).then_inc(S(f"{name}_PT"), 1)
                output(1)

            def plain_max(name, score_banks):
                return lambda n: V.tensor_reduce(negmax[:, n:n + 1], bank[score_banks[n % len(score_banks)]][:, 0:SEQ], AX.X, ALU.max,
                                                 negate=True).then_inc(S(f"{name}_nm"), 1)

            dve.wait_ge(*at("colgain_tp", 1))
            V.tensor_copy(col_gain[:, :, :].rearrange("p r k -> p (r k)"), bank[6][:, 0:5 * KD]).then_inc(S("colgain"), 1)
            dve.wait_ge(*at("colgain", 1))
            scaled("n1", x, 0)
            evac_T("n1", 0)

            def in_evac(u):
                c, n = IN_UNITS[u]
                dve.wait_ge(*at("in_mm", 2 * u + 2))
                V.tensor_copy(proj[:, 1, c:c + n], bank[(2 * u + 1) % 4][:, 0:n]).then_inc(S("in_ev1"), 1)

            in_evac(0)
            in_evac(1)
            dve.wait_ge(*at("zT_one", 1))
            dve.wait_ge(*at("zT_tp", 1))
            V.tensor_copy(zT[0:32, :], bank[4][0:32, 0:SEQ]).then_inc(S("zT_ev"), 1)
            in_evac(2)
            for t in range(TT):
                dve.wait_ge(*at("gate_ln", t + 1))
                V.scalar_tensor_tensor(la[:, t, :], bank[6 + t][:, :], 0.0, gate_tmp[:, 0, t, :], ALU.min,
                                       ALU.subtract).then_inc(S("la"), 1)
            in_evac(3)
            dve.wait_ge(*at("gqk_tp", 2))
            V.tensor_copy(gkT[:, :, :].rearrange("p r s -> p (r s)"), bank[5][:, :]).then_inc(S("gqkT"), 1)
            in_evac(4)
            dve.wait_ge(*at("gqkT", 2))
            for i4 in range(4):
                di, r = i4 // 2, i4 % 2
                dve.wait_ge(*at("sum_exp", i4 + 1))
                last = slice(63, 128, 64) if di == 0 else slice(0, 128, 64)
                link(V.tensor_copy(chunk_decay[:, i4, :].rearrange("p (t c) -> p t c", t=TT),
                                   decay_exp[:, i4, :, 1, last]))
                q = gqT[:, r, :].rearrange("p (t c) -> p t c", t=TT)
                k = gkT[:, r, :].rearrange("p (t c) -> p t c", t=TT)
                V.tensor_tensor(decay_exp[:, i4, :, 0, :], decay_exp[:, i4, :, 0, :], q, ALU.mult)
                V.tensor_tensor(decay_exp[:, i4, :, 1, :], decay_exp[:, i4, :, 1, :], q, ALU.mult)
                V.tensor_tensor(key_exp[:, i4, :, :], key_exp[:, i4, :, :], k, ALU.mult).then_inc(S("gla_qk"), 1)
            dve.wait_ge(*at("in_ev0", 5))
            for di in range(2):
                dve.wait_ge(*at("rest_exp", di + 1))
                V.tensor_tensor(key_rest[:, di, :, :], key_rest[:, di, :, :], proj[:, :, C_GK:C_GK + 256], ALU.mult
                                ).then_inc(S("key_rest"), 1)
            dve.wait_ge(*at("mask_in", 16))
            dve.wait_ge(*at("scores_zero", 1))
            for h in range(GLA_H):
                dve.wait_ge(*at("gla_sc", h + 1))
                V.copy_predicated(scores[:, h, :], gla_mask[:, :], bank[h][:, :]).then_inc(S("gla_masked"), 1)
            for n in range(3):
                for i4 in range(4):
                    ch = n if i4 < 2 else 3 - n
                    if n == 0:
                        dve.wait_ge(*at("gla_kv", 4))
                        i = V.tensor_copy(state[:, i4, 0, :], kv_of(i4, ch))
                    else:
                        i = V.scalar_tensor_tensor(state[:, i4, n, :], state[:, i4, n - 1, :],
                                                   chunk_decay[:, i4, ch:ch + 1], kv_of(i4, ch),
                                                   ALU.mult, ALU.add)
                    if n < 2 and i4 == 3:
                        link(i)
                    elif n == 2:
                        i.then_inc(S("gla_state"), 1)
            NH = GQA_H + GQA_KV
            qk = proj[:, :, C_AQ:C_AV].rearrange("p t (h d) -> p t h d", d=HD)
            dve.wait_ge(*at("gqa_sq", TT))
            V.tensor_reduce(stat[:, 16:16 + TT * NH].rearrange("p (t h) -> p t h", t=TT), gqa_tmp, AX.X, ALU.add
                            ).then_inc(S("gqa_ss"), 1)
            dve.wait_ge(*at("gqa_rstd", 1))
            r = stat[:, 16:16 + TT * NH].rearrange("p (t h) -> p t h", t=TT).unsqueeze(3).to_broadcast([P, TT, NH, HD])
            link(V.tensor_tensor(qk, qk, r, ALU.mult))
            dve.wait_ge(*at("qkgain_in", 32))
            for a, b, g in ((0, GQA_H, 0), (GQA_H, NH, HD)):
                gain = qk_gain[:, g:g + HD].unsqueeze(1).unsqueeze(1).to_broadcast([P, TT, b - a, HD])
                i = V.tensor_tensor(qk[:, :, a:b, :], qk[:, :, a:b, :], gain, ALU.mult)
            link(i)

            def table(name, n):
                return C1(name).rearrange("p (t d) -> p t d", t=TT).unsqueeze(2).to_broadcast([P, TT, NH, n])

            V.tensor_tensor(gqa_tmp[:, :, :, 0:HD:2], qk[:, :, :, 1:HD:2], table("gqa_nsin", HD // 2), ALU.mult)
            link(V.tensor_tensor(gqa_tmp[:, :, :, 1:HD:2], qk[:, :, :, 0:HD:2], table("gqa_sin", HD // 2), ALU.mult))
            link(V.tensor_tensor(qk, qk, table("gqa_cos", HD), ALU.mult))
            link(V.tensor_tensor(qk, qk, gqa_tmp, ALU.add))
            for u in range(2):
                i = V.tensor_copy(kdup[:, :, :, u, :], qk[:, :, GQA_H:NH, :])
            i.then_inc(S("gqa_qk"), 1)
            dve.wait_ge(*at("gg_silu", 1))
            sg = gate_tmp[:, 0, :, :]
            dve.wait_ge(*at("glagain_in", 16))
            sgh = sg.rearrange("p t (h d) -> p (t h) d", h=GLA_H)
            link(V.tensor_tensor(sgh, sgh, gla_gain.unsqueeze(1).to_broadcast([P, TT * GLA_H, GLA_DV]), ALU.mult))
            dve.wait_ge(*at("gla_sq", 2 * TT))
            V.tensor_reduce(stat[:, 8:16], gate_tmp[:, 1, :, :].rearrange("p t (h d) -> p (t h) d", h=GLA_H), AX.X,
                            ALU.add).then_inc(S("gla_ss"), 1)
            dve.wait_ge(*at("gqa_tp", 1))
            V.tensor_copy(gqa_kT[:, :, :].rearrange("p r s -> p (r s)"), bank[6][:, :]).then_inc(S("gqa_T"), 1)
            dve.wait_ge(*at("gla_rstd", 1))
            og = o_gla[:, :, :].rearrange("p t (h d) -> p (t h) d", h=GLA_H)
            link(V.tensor_tensor(og, og, stat[:, 8:16].unsqueeze(2).to_broadcast([P, TT * GLA_H, GLA_DV]), ALU.mult))
            link(V.tensor_tensor(mix[:, 0, 0:512], o_gla[:, 0, :], sg[:, 0, :], ALU.mult))
            link(V.tensor_tensor(mix[:, 1, 0:512], o_gla[:, 1, :], sg[:, 1, :], ALU.mult))

            def gqa_output(t):
                dve.wait_ge(*at("gqa_pv", 8 * (t + 1)))
                link(V.reciprocal(ersum[:, 8 * t:8 * t + 8], esum[:, 8 * t:8 * t + 8]))
                V.tensor_tensor(o_att[:, t, :].rearrange("p (h d) -> p h d", d=HD),
                                bank[4 + t][:, :].rearrange("p (h d) -> p h d", d=HD),
                                ersum[:, 8 * t:8 * t + 8].unsqueeze(2).to_broadcast([P, 8, HD]), ALU.mult
                                ).then_inc(S("att_o"), 1)

            attend("gqa", 16, probsT, lambda t: TT, plain_max("gqa", (0, 1, 2, 3)), 3, gqa_output)
            dve.wait_ge(*at("attgain_in", 16))
            scaled("att", o_att, 2, att_gain, mix[:, :, 512:1024], "mix_n")
            evac_T("mix")

            def add_out(name, t, u):
                xs = x[:, t, 512 * u:512 * (u + 1)]
                dve.wait_ge(*at(f"{name}_mm", 2 * t + u + 1))
                V.tensor_tensor(xs, xs, bank[(2 * u + t) % 4][:, :], ALU.add).then_inc(S(f"{name}_ev{t}"), 1)

            scaled("mm", mem, 36, dst=mem)
            dve.wait_ge(*at("norm2gain_in", 16))
            for t in range(TT):
                for u in range(2):
                    add_out("out", t, u)
                if t == 0:
                    evac_T("mm", 2, memT)
                scaled("n2", x, 4, row_gain[:, 0, :], tiles=(t,))
            evac_T("n2")

            dve.wait_ge(*at("route_mm", 1))
            for t in range(TT):
                i = V.tensor_copy(logits[:, t, :], bank[t][:, 0:72])
            link(i)
            lg, le = logits[:, :, 0:NG], logits[:, :, NG:]
            rank8 = C1("rank8").unsqueeze(1).to_broadcast([P, TT, NG])
            rank64 = C1("rank64").unsqueeze(1).to_broadcast([P, TT, NE])

            def over(v, n):
                return v.unsqueeze(2).to_broadcast([P, TT, n])

            def first_max(dst, src, n, rank, top, tmp):
                link(V.tensor_reduce(top, src, AX.X, ALU.max))
                link(V.tensor_tensor(tmp, src, over(top, n), ALU.is_equal))
                link(V.tensor_tensor(tmp, tmp, rank, ALU.mult))
                link(V.tensor_reduce(rs[11], tmp, AX.X, ALU.max))
                link(V.tensor_tensor(dst, tmp, over(rs[11], n), ALU.is_equal))

            first_max(rg[2], lg, NG, rank8, rs[0], rg[3])
            V.tensor_tensor(rg[0], lg, over(rs[0], NG), ALU.subtract).then_inc(S("route_d"), 1)
            link(V.tensor_scalar(rg[3], rg[2], -NEG, NEG, ALU.mult, ALU.add))
            link(V.tensor_tensor(rt[0].rearrange("p t (g e) -> p t g e", g=NG), le.rearrange("p t (g e) -> p t g e", g=NG),
                                 rg[3].unsqueeze(3).to_broadcast([P, TT, NG, EPG]), ALU.add))
            first_max(rt[1], rt[0], NE, rank64, rs[1], rt[2])
            link(V.scalar_tensor_tensor(rt[3].rearrange("p t e -> p (t e)"), rt[1].rearrange("p t e -> p (t e)"), -3e38,
                                        rt[0].rearrange("p t e -> p (t e)"), ALU.mult, ALU.add))
            first_max(rt[4], rt[3], NE, rank64, rs[2], rt[2])
            V.tensor_tensor(picked, rt[1], rt[4], ALU.add).then_inc(S("picked"), 1)
            V.tensor_tensor(rs[5], rs[2], rs[1], ALU.subtract).then_inc(S("route_d"), 1)
            dve.wait_ge(*at("route_e", 1))
            link(V.tensor_reduce(rs[3], rg[1], AX.X, ALU.add))
            link(V.reciprocal(rs[4], rs[3]))
            dve.wait_ge(*at("route_e", 2))
            link(V.tensor_scalar(rs[7], rs[6], 1.0, None, ALU.add))
            link(V.reciprocal(rs[8], rs[7]))
            link(V.tensor_tensor(rs[9], rs[4], rs[8], ALU.mult))
            link(V.tensor_tensor(rs[10], rs[9], rs[6], ALU.mult))
            link(V.tensor_tensor(rt[1], rt[1], over(rs[9], NE), ALU.mult))
            link(V.tensor_tensor(rt[4], rt[4], over(rs[10], NE), ALU.mult))
            link(V.tensor_tensor(gate_of, rt[1], rt[4], ALU.add))
            dve.wait_ge(*at("place_mm", 1))
            link(V.tensor_tensor(rt[0], bank[3][:, 0:2 * NE].rearrange("p (t e) -> p t e", t=TT), picked, ALU.mult))
            link(V.tensor_scalar(rt[2], picked, -1.0, None, ALU.add))
            link(V.tensor_tensor(place, rt[0], rt[2], ALU.add))
            link(V.tensor_reduce(rs[3][0:1, 0:1], bank[3][0:1, 2 * NE:3 * NE], AX.X, ALU.max))
            link(V.tensor_scalar(rounds_f[0:1, 0:7], C1("rounds")[0:1, :], rs[3][0:1, 0:1], 1.0, ALU.is_lt, ALU.add,
                                 accum_out=rounds_f[0:1, 7:8]))
            V.tensor_copy(rounds_i[0:1, 0:1], rounds_f[0:1, 7:8]).then_inc(S("rounds_ready"), 1)
            link(V.tensor_copy(slots_now, C1("slot")))

            V.memset(stat[:, 120:121], 0.0).then_inc(S("moe_xadd"), 1)
            dve.wait_ge(*at("rounds_ready", 1))
            rounds = dve.value_load(rounds_i[0:1, 0:1], min_val=1, max_val=MAX_ROUNDS)
            LINKS = TT
            with dve.Fori(0, rounds) as c:
                with dve.Fori(0, NB) as b:
                    it = c * NB + b
                    links = [0]

                    def mlink(i):
                        i.then_inc(S("moe_chain"), 1)
                        links[0] += 1
                        dve.wait_ge(*at("moe_chain", it * LINKS + links[0]))

                    for t in range(TT):
                        mlink(V.tensor_tensor(
                            sel[:, t, :].rearrange("p (q j) -> p q j", q=BATCH),
                            slots_now.unsqueeze(1).to_broadcast([P, BATCH, TOK]),
                            place[:, t, bass.ds(b * BATCH, BATCH)].unsqueeze(2).to_broadcast([P, BATCH, TOK]),
                            ALU.is_equal))
                        i = V.tensor_tensor(
                            sel_gate[:, t, :].rearrange("p (q j) -> p q j", q=BATCH),
                            sel[:, t, :].rearrange("p (q j) -> p q j", q=BATCH),
                            gate_of[:, t, bass.ds(b * BATCH, BATCH)].unsqueeze(2).to_broadcast([P, BATCH, TOK]),
                            ALU.mult)
                    i.then_inc(S("moe_sel"), 1)
                    dve.wait_ge(*at("moe_xg_mm", it * 2 + 2))
                    V.tensor_copy(xg[:, 4:8, :].rearrange("p k s -> p (k s)"), bank[3][:, :]).then_inc(S("moe_xg_v"), 1)
                    for q in range(BATCH):
                        dve.wait_ge(*at("moe_e", it * BATCH + q + 1))
                        V.tensor_tensor(hx[:, q % 2, :], eg[:, q % 2, :], bank[q % 2][:, P:2 * P], ALU.mult).then_inc(S("moe_h"), 1)
                    dve.wait_ge(*at("moe_d", it * BATCH + BATCH))
                    V.tensor_copy(y_batch[:, 512:1024], bank[7][:, :]).then_inc(S("moe_y_v"), 1)
                    for n in range(4):
                        half, t = n // 2, n % 2
                        xs = x[:, t, half * 512:(half + 1) * 512]
                        dve.wait_ge(*at("moe_cmb", it * 4 + n + 1))
                        V.tensor_tensor(xs, xs, bank[2 + n % 2][:, :], ALU.add).then_inc(S("moe_xadd"), 1)
                    assert links[0] == LINKS
                V.tensor_scalar(slots_now, slots_now, float(TOK), None, ALU.add).then_inc(S("moe_round"), 1)
                dve.wait_ge(*at("moe_round", c + 1))
            dve.wait_ge(*at("moe_xadd", rounds * (4 * NB) + 1))
            V.memset(stat[:, 121:122], 0.0).then_inc(S("moe_x"), 1)
            dve.wait_ge(*at("finalgain_in", 16))
            scaled("fin", x, 6, row_gain[:, 1, :], x, "x_final")
            def evac_odd(name, n, dst_of, bank_of, scale=None):
                for u in range(n):
                    dve.wait_ge(*at(f"{name}_mm", 2 * u + 2))
                    if scale is None:
                        i = V.tensor_copy(dst_of(u), bank_of(u))
                    else:
                        i = V.tensor_scalar(dst_of(u), bank_of(u), scale, None, ALU.mult)
                    i.then_inc(S(f"{name}_ev1"), 1)

            def two_chunks(dst, j):
                return dst[:, 2 * j:2 * j + 2, :].rearrange("p k s -> p (k s)")

            scaled("pm", x, 38)
            evac_odd("cv", 2, lambda u: c_v[:, 1, 512 * u:512 * (u + 1)], lambda u: bank[(2 * u + 1) % 4][:, :])
            evac_T("pm", 1)

            def in2_evac(u):
                dve.wait_ge(*at("in2_mm", 2 * u + 2))
                V.tensor_copy(proj2[:, 1, IN2_UNITS[u]:IN2_UNITS[u] + 512], bank[(2 * u + 1) % 4][:, :]
                              ).then_inc(S("in2_ev1"), 1)

            for u in range(3):
                in2_evac(u)
            dve.wait_ge(*at("in2_ev0", 3))
            dve.wait_ge(*at("in2_ev1", 3))
            dve.wait_ge(*at("c2_in", 16))
            for c0, nh, hw, name in ((C_MQ, 2 * MOBA_H, 8, "moba"), (C_RQ, 2 * RET_H, 32, "ret")):
                v = proj2[:, :, c0:c0 + nh * HD].rearrange("p t (h d) -> p t h d", d=HD)
                lo, hi = v[:, :, :, 0:hw], v[:, :, :, hw:2 * hw]
                cos, sin = (C2(f"{name}_{f}").rearrange("p (t d) -> p t d", t=TT).unsqueeze(2)
                            .to_broadcast([P, TT, nh, hw]) for f in ("cos", "sin"))
                tmp = [rope_tmp[:, n, :, 0:nh * hw].rearrange("p t (h d) -> p t h d", d=hw) for n in range(4)]
                if name == "ret":
                    dve.wait_ge(*at("rope", 1))
                for n, (a, b) in enumerate(((lo, cos), (hi, sin), (hi, cos), (lo, sin))):
                    i = V.tensor_tensor(tmp[n], a, b, ALU.mult)
                link(i)
                link(V.tensor_tensor(lo, tmp[0], tmp[1], ALU.subtract))
                V.tensor_tensor(hi, tmp[2], tmp[3], ALU.add).then_inc(S("rope"), 1)
                in2_evac(3 if name == "moba" else 4)
            dve.wait_ge(*at("r_tp", 2))
            V.tensor_copy(two_chunks(r_kT, 0), bank[1][:, :]).then_inc(S("r_T"), 1)
            in2_evac(5)
            W = SEQ + P
            for h in range(RET_H):
                dve.wait_ge(*at("ret_sc", h + 1))
                V.tensor_tensor(r_scores[:, h, :], bank[h][:, 0:W], C2("decay", h * W, (h + 1) * W), ALU.mult
                                ).then_inc(S("ret_decayed"), 1)
            for r in range(2):
                dve.wait_ge(*at("m_tp", 3 + r))
                V.tensor_copy(two_chunks(m_kT, r), bank[6 + r][:, :]).then_inc(S("m_T"), 1)
            dve.wait_ge(*at("ret_sq", TT))
            V.tensor_reduce(stat[:, 40:48], r_square[:, :, :].rearrange("p t (h d) -> p (t h) d", h=RET_H), AX.X,
                            ALU.add).then_inc(S("ret_ss"), 1)
            dve.wait_ge(*at("ret_ss", 1))
            def ret_output():
                dve.wait_ge(*at("ret_rstd", 1))
                ro = ret_o[:, :, :].rearrange("p t (h d) -> p (t h) d", h=RET_H)
                dve.wait_ge(*at("ret_oc", TT))
                link(V.tensor_tensor(ro, ro, stat[:, 40:48].unsqueeze(2).to_broadcast([P, TT * RET_H, RET_DV]), ALU.mult))
                dve.wait_ge(*at("rg_silu", 1))
                link(V.tensor_tensor(mix[:, :, 512:1024], ret_o, ret_g, ALU.mult))

            def masked_max(n):
                w = (n // MOBA_H + 1) * P
                link(V.tensor_tensor_reduce(m_probs[:, n % 3, 0:w], bank[(2, 3, 0, 1)[n % 4]][:, 0:w], C2("causal", 2 * P - w, 2 * P),
                                            1.0, -3e38, ALU.add, ALU.max, ersum[:, n:n + 1]))
                V.tensor_scalar(negmax[:, n:n + 1], ersum[:, n:n + 1], -1.0, None, ALU.mult).then_inc(S("moba_nm"), 1)

            def moba_output(t):
                if t == 0:
                    ret_output()
                dve.wait_ge(*at("moba_pv", MOBA_H * (t + 1)))
                link(V.reciprocal(ersum[:, 8 * t:8 * t + 8], esum[:, 8 * t:8 * t + 8]))
                V.tensor_tensor(mix[:, t, 0:512].rearrange("p (h d) -> p h d", d=HD),
                                bank[4 + t][:, :].rearrange("p (h d) -> p h d", d=HD),
                                ersum[:, 8 * t:8 * t + 8].unsqueeze(2).to_broadcast([P, 8, HD]), ALU.mult
                                ).then_inc(S("mix2_n"), 1)

            attend("moba", 16, probsT2, lambda t: t + 1, masked_max, 2, moba_output)
            evac_T("mix2")

            def y_half(name, bank_of):
                for u in range(2):
                    dve.wait_ge(*at(f"{name}_mm", 2 + u + 1))
                    V.tensor_copy(y[:, 1, 512 * u:512 * (u + 1)], bank_of(u)[:, :]).then_inc(S(f"{name}_ev1"), 1)

            def add_normed(of, col, row, signal, t):
                dve.wait_ge(*at(f"{of}_rstd", t + 1))
                link(V.scalar_tensor_tensor(y[:, t, :], y[:, t, :], stat[:, col + t:col + t + 1], row_gain[:, row, :],
                                            ALU.mult, ALU.mult))
                V.tensor_tensor(x[:, t, :], x[:, t, :], y[:, t, :], ALU.add).then_inc(S(signal), 1)

            def y_and_next(name, of, col, row, nx, next_col, gain):
                for t in range(TT):
                    if t == 1:
                        y_half(name, lambda u: bank[(2 * u + 1) % 4])
                    add_normed(of, col, row, f"{of}_x", t)
                    scaled(nx, x, next_col, tiles=(t,))
                    evac_T(nx, gain, tiles=(t,))

            dve.wait_ge(*at("postmix_in", 16))
            y_and_next("out2", "om", 48, 0, "pc", 50, 3)
            evac_odd("cq", 2, lambda u: two_chunks(c_qT, 2 * u + 1), lambda u: bank[2 * u + 1][:, :], CROSS_D ** -0.5)

            def cross_output(t):
                dve.wait_ge(*at("cross_pv", CROSS_H * (t + 1)))
                link(V.reciprocal(ersum[:, 4 * t:4 * t + 4], esum[:, 4 * t:4 * t + 4]))
                for r in range(2):
                    i = V.tensor_tensor(mix[:, t, 512 * r:512 * (r + 1)].rearrange("p (h d) -> p h d", h=2),
                                        bank[(4 if t == 0 else 0) + r][:, :].rearrange("p (h d) -> p h d", h=2),
                                        ersum[:, 4 * t + 2 * r:4 * t + 2 * r + 2].unsqueeze(2)
                                        .to_broadcast([P, 2, CROSS_D]), ALU.mult)
                i.then_inc(S("cmix_n"), 1)

            attend("cross", 8, probsT2, lambda t: TT, plain_max("cross", (2, 3)), 1, cross_output)
            evac_T("cmix")
            dve.wait_ge(*at("postcross_in", 16))
            y_and_next("co", "oc", 52, 1, "pf", 54, 4)
            for j in range(KF):
                dve.wait_ge(*at("ff_silu", j + 1))
                V.tensor_tensor(ffT[:, j, :], ff_e[:, j % 4, :], bank[j % 4][:, SEQ:2 * SEQ], ALU.mult).then_inc(S("ff_h"), 1)
            dve.wait_ge(*at("postffn_in", 16))
            for t in range(TT):
                if t == 1:
                    y_half("down", lambda u: bank[5 + 2 * u])
                add_normed("of", 56, 0, "ffn_x", t)


_INS = ["x", "norm1_gain", "w_in", "gla_up_fwd", "gla_up_fwd_bias", "gla_up_bwd", "gla_up_bwd_bias", "gla_out_gain",
        "q_norm_gain", "k_norm_gain", "att_out_gain", "w_out", "norm2_gain", "w_group", "b_group", "w_expert",
        "b_expert", "w_gate", "w_up", "w_down", "final_gain", "mem_2", "g_pre_mix_2", "w_in_2", "w_out_2",
        "g_post_mix_2", "g_pre_cross_2", "g_mem_2", "w_cq_2", "w_ckv_2", "w_co_2", "g_post_cross_2", "g_pre_ffn_2",
        "w_gate_up_2", "w_down_2", "g_post_ffn_2"]


def kernel(**inputs):
    import concourse.bacc as _bacc
    from concourse.bass_utils import run_bass_kernel_spmd as _run

    nc = _bacc.Bacc("TRN2", target_bir_lowering=False, num_devices=1)
    arrays, t_in = {}, {}

    def dram(name, a):
        arrays[name] = a
        return nc.dram_tensor(name, a.shape, mybir.dt.from_np(a.dtype), kind="ExternalInput").ap()

    for name in _INS:
        t_in[name] = dram(f"in_{name}_dram", np.ascontiguousarray(inputs[name]))
    c1, c1_at, c2, c2_at, mask = shape_constants()
    consts = {"c1": dram("const_1", c1), "c2": dram("const_2", c2), "mask": dram("const_mask", mask),
              "c1_at": c1_at, "c2_at": c2_at}
    out = nc.dram_tensor("out_0_dram", (1, SEQ, D), F32, kind="ExternalOutput").ap()
    build(nc, t_in, consts, out)
    r = _run(nc, [arrays], core_ids=[0])
    return r.results[0]["out_0_dram"]
```
